# Optimizing a Trainium2 kernel written in Bass

```python
import math
import jax, jax.numpy as jnp
from jax import lax
import numpy as np

D_MODEL = 1024
BATCH = 1
SEQ = 512
DEPTH = 2

ROPE_THETA = 10000.0
NORM_EPS = 1e-6

BRANCH_W = D_MODEL // 2
N_BRANCH = 3

GLA_HEADS = 4
GLA_DV = BRANCH_W // GLA_HEADS
GLA_DK = GLA_DV // 2
GLA_RANK = 16
GLA_TAU = 16.0
GLA_CHUNK = 64
GLA_QK_W = GLA_HEADS * GLA_DK

DIFF_HEADS = 4
DIFF_D = BRANCH_W // (2 * DIFF_HEADS)
DIFF_QK_W = DIFF_HEADS * 2 * DIFF_D
DIFF_QBLOCK = 128

DIL_HEADS = 8
DIL_HD = BRANCH_W // DIL_HEADS
DIL_W = DIL_HEADS * DIL_HD
DIL_PATTERNS = ((128, 1), (512, 4), (2048, 16))
DIL_QBLOCK = 64

IN_SPLITS = (
    GLA_QK_W, GLA_QK_W, BRANCH_W, BRANCH_W, GLA_RANK, GLA_RANK,
    DIFF_QK_W, DIFF_QK_W, BRANCH_W, BRANCH_W,
    DIL_W, DIL_W, BRANCH_W, BRANCH_W,
    N_BRANCH * D_MODEL,
)
IN_COLS = sum(IN_SPLITS)

kernel_name = "hybrid_gla_diff_dilated_encoder"

def rms_norm(x, g):
    xf = x.astype(jnp.float32)
    y = xf * lax.rsqrt(jnp.mean(xf * xf, axis=-1, keepdims=True) + NORM_EPS)
    return (y * g.astype(jnp.float32)).astype(x.dtype)

def rope_tables(seq, dim):
    inv = 1.0 / (ROPE_THETA ** (jnp.arange(0, dim, 2, dtype=jnp.float32) / dim))
    ang = jnp.arange(seq, dtype=jnp.float32)[:, None] * inv[None, :]
    return jnp.cos(ang), jnp.sin(ang)

def apply_rope(x, cos, sin):
    x1, x2 = jnp.split(x.astype(jnp.float32), 2, axis=-1)
    return jnp.concatenate([x1 * cos - x2 * sin, x2 * cos + x1 * sin], axis=-1).astype(x.dtype)

def split_points():
    pts, acc = [], 0
    for s in IN_SPLITS[:-1]:
        acc += s
        pts.append(acc)
    return pts

def gla_one_direction(q, k, v, log_a):
    B, H, S, DK = q.shape
    DV = v.shape[-1]
    C = GLA_CHUNK
    N = S // C
    q = q.reshape(B, H, N, C, DK)
    k = k.reshape(B, H, N, C, DK)
    v = v.reshape(B, H, N, C, DV)
    b = jnp.cumsum(log_a.reshape(B, H, N, C, DK), axis=3)
    b_last = b[:, :, :, -1:, :]
    q_hat = q * jnp.exp(b)
    k_hat = k * jnp.exp(-b)
    tri = jnp.tril(jnp.ones((C, C), dtype=bool))
    att = jnp.where(tri, jnp.einsum('bhncd,bhnjd->bhncj', q_hat, k_hat), 0.0)
    o_intra = jnp.einsum('bhncj,bhnje->bhnce', att, v)
    k_end = k * jnp.exp(b_last - b)
    upd = jnp.einsum('bhncd,bhnce->nbhde', k_end, v)
    decay = jnp.moveaxis(jnp.exp(b_last[:, :, :, 0, :]), 2, 0)[..., None]

    def step(state, inp):
        d, u = inp
        return d * state + u, state

    _, s_in = lax.scan(step, jnp.zeros((B, H, DK, DV), q.dtype), (decay, upd))
    o_inter = jnp.einsum('bhncd,nbhde->bhnce', q_hat, s_in)
    return (o_intra + o_inter).reshape(B, H, S, DV)

def diff_attention(q, k, v, lam):
    B, H, _, S, d = q.shape
    nb = S // DIFF_QBLOCK
    qb = jnp.moveaxis(q.reshape(B, H, 2, nb, DIFF_QBLOCK, d), 3, 0)
    scale = d ** -0.5

    def block(qblk):
        s = jnp.einsum('bhtqd,bhtkd->bhtqk', qblk, k, preferred_element_type=jnp.float32) * scale
        p = jax.nn.softmax(s, axis=-1)
        w = p[:, :, 0] - lam * p[:, :, 1]
        return jnp.einsum('bhqk,bhke->bhqe', w.astype(v.dtype), v)

    o = lax.map(block, qb)
    return jnp.moveaxis(o, 0, 2).reshape(B, H, S, 2 * d)

def dilated_window_attention(q, k, v, dilation, half):
    B, H, S, hd = q.shape
    Sr = S // dilation
    bq = math.gcd(DIL_QBLOCK, Sr)
    nb = Sr // bq
    L = bq + 2 * half

    def to_classes(t):
        return t.reshape(B, H, Sr, dilation, hd).transpose(0, 1, 3, 2, 4)

    qc, kc, vc = to_classes(q), to_classes(k), to_classes(v)
    pad = ((0, 0), (0, 0), (0, 0), (half, half), (0, 0))
    kp = jnp.pad(kc, pad)
    vp = jnp.pad(vc, pad)
    idx = (jnp.arange(nb) * bq)[:, None] + jnp.arange(L)[None, :]
    kb = kp[:, :, :, idx, :]
    vb = vp[:, :, :, idx, :]
    qb = qc.reshape(B, H, dilation, nb, bq, hd)
    s = jnp.einsum('bhrnqd,bhrnld->bhrnql', qb, kb, preferred_element_type=jnp.float32) * (hd ** -0.5)
    rel = jnp.arange(L)[None, :] - half - jnp.arange(bq)[:, None]
    src = idx[:, None, :] - half
    valid = (jnp.abs(rel) <= half)[None] & (src >= 0) & (src < Sr)
    s = jnp.where(valid, s, -1e30)
    lse = jax.nn.logsumexp(s, axis=-1)
    p = jnp.exp(s - lse[..., None])
    o = jnp.einsum('bhrnql,bhrnld->bhrnqd', p.astype(v.dtype), vb)
    o = o.reshape(B, H, dilation, Sr, hd).transpose(0, 1, 3, 2, 4).reshape(B, H, S, hd)
    lse = lse.reshape(B, H, dilation, Sr).transpose(0, 1, 3, 2).reshape(B, H, S)
    return o, lse

def hybrid_layer(x, layer, cos_b, sin_b, cos_c, sin_c, norm_g, w_in, gla_gate_up, gla_gate_b,
                 gla_norm_g, diff_lambda, diff_norm_g, w_branch, w_out):
    B, S, _ = x.shape
    f32 = jnp.float32
    h = rms_norm(x, norm_g)
    proj = jnp.einsum('bsd,dc->bsc', h, w_in)
    (a_q, a_k, a_v, a_g, a_lf, a_lb,
     b_q, b_k, b_v, b_g,
     c_q, c_k, c_v, c_g, merge) = jnp.split(proj, split_points(), axis=-1)

    def heads(t, n):
        return t.reshape(B, S, n, -1).transpose(0, 2, 1, 3)

    qa = heads(a_q, GLA_HEADS).astype(f32) * (GLA_DK ** -0.5)
    ka = heads(a_k, GLA_HEADS).astype(f32)
    va = heads(a_v, GLA_HEADS).astype(f32)
    la_f = heads(jax.nn.log_sigmoid((a_lf @ gla_gate_up[0] + gla_gate_b[0]).astype(f32)) / GLA_TAU, GLA_HEADS)
    la_b = heads(jax.nn.log_sigmoid((a_lb @ gla_gate_up[1] + gla_gate_b[1]).astype(f32)) / GLA_TAU, GLA_HEADS)
    flip = lambda t: jnp.flip(t, axis=2)
    o_a = gla_one_direction(qa, ka, va, la_f) + flip(gla_one_direction(flip(qa), flip(ka), flip(va), flip(la_b)))
    o_a = rms_norm(o_a.transpose(0, 2, 1, 3), gla_norm_g).reshape(B, S, BRANCH_W).astype(x.dtype)
    y_a = o_a * jax.nn.silu(a_g)

    qb = apply_rope(b_q.reshape(B, S, DIFF_HEADS, 2, DIFF_D).transpose(0, 2, 3, 1, 4), cos_b, sin_b)
    kb = apply_rope(b_k.reshape(B, S, DIFF_HEADS, 2, DIFF_D).transpose(0, 2, 3, 1, 4), cos_b, sin_b)
    vb = heads(b_v, DIFF_HEADS)
    lam_init = 0.8 - 0.6 * math.exp(-0.3 * layer)
    dl = diff_lambda.astype(f32)
    lam = jnp.exp(jnp.sum(dl[0] * dl[1])) - jnp.exp(jnp.sum(dl[2] * dl[3])) + lam_init
    o_b = diff_attention(qb, kb, vb, lam)
    o_b = rms_norm(o_b.transpose(0, 2, 1, 3), diff_norm_g) * (1.0 - lam_init)
    y_b = o_b.reshape(B, S, BRANCH_W).astype(x.dtype) * jax.nn.silu(b_g)

    qc = apply_rope(heads(c_q, DIL_HEADS), cos_c, sin_c)
    kc = apply_rope(heads(c_k, DIL_HEADS), cos_c, sin_c)
    vc = heads(c_v, DIL_HEADS)
    outs, lses = [], []
    for window, dil in DIL_PATTERNS:
        o_g, lse_g = dilated_window_attention(qc, kc, vc, dil, window // (2 * dil))
        outs.append(o_g)
        lses.append(lse_g)
    wts = jax.nn.softmax(jnp.stack(lses, axis=0), axis=0)
    o_c = jnp.einsum('gbhs,gbhsd->bhsd', wts, jnp.stack(outs, axis=0).astype(f32))
    y_c = o_c.transpose(0, 2, 1, 3).reshape(B, S, BRANCH_W).astype(x.dtype) * jax.nn.silu(c_g)

    y = jnp.stack([y_a, y_b, y_c], axis=2)
    z = jnp.einsum('bsgw,gwd->bsgd', y, w_branch)
    gates = jax.nn.sigmoid(merge.reshape(B, S, N_BRANCH, D_MODEL))
    mixed = jnp.sum(gates * z, axis=2)
    return x + jnp.einsum('bsd,de->bse', mixed, w_out)

def setup_inputs(seed: int = 0) -> dict:
    key = jax.random.key(seed)
    ks = jax.random.split(key, 12)
    nrm = jax.random.normal
    return {
        "x": nrm(ks[0], (BATCH, SEQ, D_MODEL), jnp.float32),
        "norm_g": 1.0 + 0.02 * nrm(ks[1], (DEPTH, D_MODEL), jnp.float32),
        "w_in": nrm(ks[2], (DEPTH, D_MODEL, IN_COLS), jnp.float32) * D_MODEL ** -0.5,
        "gla_gate_up": nrm(ks[3], (DEPTH, 2, GLA_RANK, GLA_QK_W), jnp.float32) * GLA_RANK ** -0.5,
        "gla_gate_b": 0.02 * nrm(ks[4], (DEPTH, 2, GLA_QK_W), jnp.float32),
        "gla_norm_g": 1.0 + 0.02 * nrm(ks[5], (DEPTH, GLA_DV), jnp.float32),
        "diff_lambda": 0.1 * nrm(ks[6], (DEPTH, 4, DIFF_D), jnp.float32),
        "diff_norm_g": 1.0 + 0.02 * nrm(ks[7], (DEPTH, 2 * DIFF_D), jnp.float32),
        "w_branch": nrm(ks[8], (DEPTH, N_BRANCH, BRANCH_W, D_MODEL), jnp.float32) * BRANCH_W ** -0.5,
        "w_out": nrm(ks[9], (DEPTH, D_MODEL, D_MODEL), jnp.float32) * D_MODEL ** -0.5,
        "final_norm_g": 1.0 + 0.02 * nrm(ks[10], (D_MODEL,), jnp.float32),
    }

def reference(x, norm_g, w_in, gla_gate_up, gla_gate_b, gla_norm_g, diff_lambda, diff_norm_g,
              w_branch, w_out, final_norm_g):
    S = x.shape[1]
    cos_b, sin_b = rope_tables(S, DIFF_D)
    cos_c, sin_c = rope_tables(S, DIL_HD)
    for layer in range(DEPTH):
        x = hybrid_layer(x, layer, cos_b, sin_b, cos_c, sin_c, norm_g[layer], w_in[layer],
                         gla_gate_up[layer], gla_gate_b[layer], gla_norm_g[layer],
                         diff_lambda[layer], diff_norm_g[layer], w_branch[layer], w_out[layer])
    return rms_norm(x, final_norm_g)


_drawn_inputs = setup_inputs


def setup_inputs(seed=0):
    import zlib

    import numpy as np

    out = dict(_drawn_inputs(seed))
    spreads = {}
    factors = {'gla_gate_b': 8.0, 'gla_norm_g': 6.054, 'diff_norm_g': 8.0, 'final_norm_g': 2.918}
    for name, (base, spread) in spreads.items():
        noise = np.random.default_rng([zlib.crc32(name.encode()), seed]).standard_normal(out[name].shape)
        drawn = base * np.exp(spread * noise) if base else spread * noise
        out[name] = __import__('jax').numpy.asarray(drawn.astype(out[name].dtype))
    for name, factor in factors.items():
        out[name] = (out[name] * factor).astype(out[name].dtype)
    return out
```

```python
import math
from contextlib import ExitStack

import numpy as np

import concourse.bass as bass
from concourse import mybir

F32 = mybir.dt.float32
U32 = mybir.dt.uint32
ACT = mybir.ActivationFunctionType
ALU = mybir.AluOpType
AX_X = mybir.AxisListType.X

P = 128
DEPTH, S, D = 2, 512, 1024
KT = D // P
QB = S // P
NG = 4
BW = 512
DK, DV = 64, 128
RANK = 16
CH = 64
NC = S // CH
HD = 64
THETA, EPS = 10000.0, 1e-6
PATTERNS = ((128, 1), (512, 4), (2048, 16))
TAU = 16.0

TILES = ["v0", "v1", "v2", "v3", "aq", "ak", "bq", "bk", "cq", "ck", "ag", "bg", "cg",
         "m0", "m1", "m2", "m3", "sumB", "m4", "m5"]
NT = len(TILES)
T = {name: n for n, name in enumerate(TILES)}
UNIT_TILES = [n for n in TILES[4:] if n != "sumB"]
GU = 3 + len(UNIT_TILES)
ROWS_LAYER = NG * GU + 12 + 8
RING = 6
LAYER_TILES = NG * NT + 24 + 8
SLOT_USES = [16] * 4 + [14] * 2
BY_DVE = ["aq", "ak", "ag", "bg", "cg"]
BY_ACT = [n for n in TILES if n not in BY_DVE]

C_LOW, C_UP, C_GB, C_NG = 0, 256, 768, 772
C_GA, C_GD, C_DL, C_LI, NPAR = 780, 781, 782, 1038, 1040


class Signal:

    def __init__(self, sem, per, credit=0):
        self.sem, self.per, self.credit = sem, per, credit

    def at(self, n, k):
        return self.sem, n * self.per + (self.credit + k)


class Chain:

    def __init__(self, eng, steps, n):
        self.eng, self.steps, self.n, self.k = eng, steps, n, 0

    def did(self, ins):
        ins.then_inc(self.steps.sem, 1)
        self.k += 1
        return self.k

    def need(self, k):
        self.eng.wait_ge(*self.steps.at(self.n, k))

    def last(self):
        self.need(self.k)

    def close(self):
        assert self.k == self.steps.per, (self.k, self.steps.per)


def freed_by(u):
    return 4 if u < 3 else T[UNIT_TILES[u - 3]] + 1


def unit_of(j):
    return j // 2 if j < 8 else j - 4


def build(nc, x_d, w_d, par_d, fin_d, cos_d, sin_d, lmask_d, cmask_d, gmask_d, ident_d, out_d, gate_d):
    with ExitStack() as ctx:
        def sb(name, shape, dt=F32):
            return ctx.enter_context(nc.sbuf_tensor(name, shape, dt))

        def bank(name):
            return ctx.enter_context(nc.psum_tensor(name, [P, S], F32))

        def sig(name, per, credit=0):
            return Signal(ctx.enter_context(nc.semaphore(name)), per, credit)

        x = sb("x", [P, KT, S])
        h = sb("h", [P, KT, S])
        y = sb("y", [P, 3 * NG, S])
        rx = sb("rx", [P, S])
        ring = sb("ring", [P, RING, 8, P])
        par = sb("par", [P, NPAR])
        sc = sb("sc", [P, 8])
        junk = sb("junk", [P, HD])
        v = sb("v", [P, QB, 3 * P])
        raw = sb("raw", [P, 2, S])
        rot = sb("rot", [P, 2, S])
        qk = sb("qk", [P, 4, S])
        la = sb("la", [P, NG, S])
        low = sb("low", [2 * RANK, S])
        cum = sb("cum", [P, S])
        rest = sb("rest", [P, S])
        qhat = sb("qhat", [P, S])
        total = sb("total", [P, NC])
        decay = sb("decay", [P, NC])
        kend = sb("kend", [P, QB, P])
        att = sb("att", [P, 2, S])
        state = sb("state", [P, NC, DV])
        sg = sb("sg", [P, 3, S])
        six = sb("six", [P, 6, S])
        probs, sneg = six[:, 0:4, :], six[:, 4:6, :]
        w = sb("w", [P, 2, S])
        wt = sb("wt", [P, QB, S])
        sq = sb("sq", [P, 2, S])
        rr = sb("rr", [P, 2, S])
        negmax = sb("negmax", [P, 16])
        sums = sb("sums", [P, 16])
        rs = sb("rs", [P, 16])
        gstage = sb("gstage", [P, 3, S])
        gates = six[:, :, :].rearrange("p (n g) s -> p n g s", n=2)
        za = sb("za", [P, 2, S])
        cos = sb("cos", [P, S])
        sin = sb("sin", [P, S])
        lmask = sb("lmask", [P, QB, S])
        cmask = sb("cmask", [P, S])
        gmask = sb("gmask", [P, 2, P], U32)
        ident = sb("ident", [P, P])
        mean = sb("mean", [P, 2, P])
        cst = sb("cst", [P, 2])
        fin = sb("fin", [P, KT])

        proj = [bank("proj0"), bank("proj1")]
        score = [bank("score0"), bank("score1")]
        turn = [bank("turn0"), bank("turn1")]
        obank, mbank = bank("obank"), bank("mbank")
        zbanks = score + turn + [obank, mbank]

        s_x, s_const = sig("s_x", 16), sig("s_const", 16 * 7)
        s_par = sig("s_par", 16)
        loaded = [sig(f"loaded{s}", 16 * SLOT_USES[s]) for s in range(RING)]
        s_init = sig("s_init", 0)
        s_passed = sig("s_passed", 0)
        tile_done = sig("tile_done", LAYER_TILES, LAYER_TILES)
        xsum_done = sig("xsum_done", 1)
        low_done = sig("low_done", 1)
        gate_done = sig("gate_done", 4)
        glaatt_done = sig("glaatt_done", 1)
        kturn_done = sig("kturn_done", 1)
        upd_done = sig("upd_done", 1)
        score_done = sig("score_done", 16)
        turn_done = sig("turn_done", 12)
        pv_done = sig("pv_done", 1)
        out_done = sig("out_done", 4)
        act_free = sig("act_free", len(BY_ACT) * NG, 1)
        xsq_done = sig("xsq_done", 4)
        xr_done = sig("xr_done", 1)
        act_pre = sig("act_pre", 9)
        low_ready = sig("low_ready", 1)
        soft_ready = sig("soft_ready", 1)
        lam_exp = sig("lam_exp", 1)
        decay_done = sig("decay_done", 4)
        tanh_done = sig("tanh_done", 3)
        kend_ready = sig("kend_ready", 1)
        exp_done = sig("exp_done", 16)
        wt_ready = sig("wt_ready", 12, 1)
        sq_done = sig("sq_done", 2)
        r_done = sig("r_done", 1)
        act_grp = sig("act_grp", 1)
        dve_free = sig("dve_free", len(BY_DVE) * NG)
        dve_pre = sig("dve_pre", 6)
        min_done = sig("min_done", NG)
        h_ready = sig("h_ready", 8)
        la_ready = sig("la_ready", 1)
        cum_ready = sig("cum_ready", 1)
        qk_ready = sig("qk_ready", 2)
        att_ready = sig("att_ready", 1)
        state_ready = sig("state_ready", 1)
        max_ready = sig("max_ready", 16)
        w_ready = sig("w_ready", 12)
        y_read = sig("y_read", 3, 1)
        dve_grp = sig("dve_grp", 42)
        z_read = sig("z_read", 24, 6)
        mixed = sig("mixed", 8, 2)
        dve_mix = sig("dve_mix", 8)
        x_ready = sig("x_ready", 8, 8)
        out_ready = sig("out_ready", 8)
        swapped = sig("swapped", 2 * 64)
        gstored = [sig(f"gstored{s}", 2 * 16, 16) for s in range(3)]
        gloaded = [sig(f"gloaded{s}", 4 * 16) for s in range(2)]
        s_out = sig("s_out", 16)

        block = ctx.enter_context(nc.Block())

        def free_of(name, L, i):
            if name in BY_DVE:
                return dve_free.at(L, len(BY_DVE) * i + (BY_DVE.index(name) + 1))
            return act_free.at(L, len(BY_ACT) * i + (BY_ACT.index(name) + 1))

        def apart(eng):
            eng.sem_inc(s_passed.sem, 1)

        @block.sync
        def _(sp):
            sp.dma_start(x[:, :, :], x_d).then_inc(s_x.sem, 16)

            def unit(L, row, slot):
                sp.dma_start(ring[:, slot, :, :], w_d[L * ROWS_LAYER + row, :, :].rearrange(
                    "p (t c) -> p t c", c=P)).then_inc(loaded[slot].sem, 16)

            with sp.Fori(0, DEPTH) as L:
                sp.wait_ge(*y_read.at(L * NG, 0))
                sp.dma_start(par[:, :], par_d[L, :, :]).then_inc(s_par.sem, 16)
                for s in range(RING):
                    last = NG * NT + (24 + 4 + s + 1 if s < 4 else 2 * (6 + s + 1))
                    sp.wait_ge(*tile_done.at(L, last - LAYER_TILES))
                    unit(L, s, s)
                with sp.Fori(0, NG) as i:
                    for j in range(GU):
                        sp.wait_ge(*tile_done.at(L, i * NT + freed_by(j)))
                        unit(L, i * GU + (RING + j), j % RING)
                for c in range(6, 12):
                    sp.wait_ge(*tile_done.at(L, NG * NT + 2 * (c - 5)))
                    unit(L, NG * GU + c, c % RING)
                for o in range(8):
                    sp.wait_ge(*tile_done.at(L, NG * NT + (2 * (7 + o) if o < 4 else 24 + o - 3)))
                    unit(L, NG * GU + 12 + o, o % 4)
            sp.wait_ge(*out_ready.at(0, 8))
            sp.dma_start(out_d, h[:, :, :]).then_inc(s_out.sem, 16)
            sp.wait_ge(*s_out.at(0, 16))

        @block.gpsimd
        def _(pool):
            for dst, src in ((cos[:, :], cos_d), (sin[:, :], sin_d), (lmask[:, :, :], lmask_d), (cmask[:, :], cmask_d),
                             (gmask[:, :, :], gmask_d), (ident[:, :], ident_d), (fin[:, :], fin_d)):
                pool.dma_start(dst, src).then_inc(s_const.sem, 16)
            with pool.Fori(0, DEPTH) as L:
                for s in range(3):
                    pool.wait_ge(*gstored[s].at((L + 1) * NG, 0))
                pool.wait_ge(*y_read.at((L + 1) * NG, 0))
                for d in range(KT):
                    pool.wait_ge(*mixed.at(L, d - 1))
                    apart(pool)
                    pool.dma_start(gates[:, d % 2, :, :], gate_d[3 * d:3 * d + 3, :, :].rearrange(
                        "g p s -> p g s")).then_inc(gloaded[d % 2].sem, 16)
                for s in range(2):
                    pool.wait_ge(*gloaded[s].at(L + 1, 0))

        @block.scalar
        def _(act):
            act.sem_inc(act_free.sem, 1)
            act.sem_inc(wt_ready.sem, 1)
            for s in range(3):
                act.sem_inc(gstored[s].sem, 16)
            act.wait_ge(*s_x.at(0, 16))
            act.wait_ge(*s_init.at(0, 1))

            def mean_square_of_x(L):
                act.wait_ge(*x_ready.at(L, 0))
                for c in range(4):
                    act.activation(h[:, 2 * c:2 * c + 2, :], x[:, 2 * c:2 * c + 2, :], ACT.Square).then_inc(xsq_done.sem, 1)

            with act.Fori(0, DEPTH) as L:
                chain = Chain(act, act_pre, L)
                act.wait_ge(*y_read.at(L * NG, 0))
                mean_square_of_x(L)
                act.wait_ge(*xsum_done.at(L, 1))
                chain.did(act.activation(rx[:, :], proj[0][:, :], ACT.Ln, bias=cst[:, 0:1]))
                chain.last()
                act.activation(rx[:, :], rx[:, :], ACT.Exp, scale=-0.5).then_inc(xr_done.sem, 1)
                act.wait_ge(*dve_pre.at(L, 2))
                act.activation(sc[:, 0:2], sc[:, 0:2], ACT.Exp).then_inc(lam_exp.sem, 1)
                act.wait_ge(*low_done.at(L, 1))
                act.activation(low[:, :], proj[1][0:2 * RANK, :], ACT.Copy).then_inc(low_ready.sem, 1)
                for hd in range(NG):
                    act.wait_ge(*min_done.at(L, hd + 1))
                    chain.did(act.activation(wt[:, hd, :], zbanks[hd][:, :], ACT.Abs, bias=par[:, C_GB + hd:C_GB + hd + 1]))
                chain.last()
                for hd in range(NG):
                    k = chain.did(act.activation(wt[:, hd, :], wt[:, hd, :], ACT.Exp, scale=-1.0))
                chain.need(k)
                act.activation(wt[:, :, :], wt[:, :, :], ACT.Ln, bias=cst[:, 1:2]).then_inc(soft_ready.sem, 1)
                chain.close()

                with act.Fori(0, NG) as i:
                    G = L * NG + i
                    grp = Chain(act, act_grp, G)
                    act.wait_ge(*y_read.at(G, 0))

                    def have(name):
                        act.wait_ge(*tile_done.at(L, i * NT + (T[name] + 1)))

                    def free(ins):
                        return ins.then_inc(act_free.sem, 1)

                    act.wait_ge(*cum_ready.at(G, 1))
                    act.activation(qhat[:, :], cum[:, :], ACT.Exp, scale=1 / TAU).then_inc(decay_done.sem, 1)
                    act.activation(rest[:, :], rest[:, :], ACT.Exp, scale=1 / TAU).then_inc(decay_done.sem, 1)
                    act.activation(decay[:, :], total[:, :], ACT.Exp, scale=1 / TAU).then_inc(decay_done.sem, 1)
                    act.wait_ge(*decay_done.at(G, 1))
                    act.activation(cum[:, :], cum[:, :], ACT.Exp, scale=-1 / TAU).then_inc(decay_done.sem, 1)
                    for b in range(QB):
                        have(f"v{b}")
                        free(act.activation(v[:, b, :], proj[b % 2][:, 0:3 * P], ACT.Copy))
                    for n, (q, k) in enumerate((("bq", "bk"), ("cq", "ck"))):
                        for m, name in enumerate((q, k)):
                            have(name)
                            if n:
                                act.wait_ge(*qk_ready.at(G, 1))
                            free(act.activation(raw[:, m, :], proj[T[name] % 2][:, :], ACT.Copy))
                        act.wait_ge(*free_of(k, L, i))
                        for a in range(4):
                            b = a ^ 1
                            act.dma_start(rot[32 * a:32 * a + 32, :, :], raw[32 * b:32 * b + 32, :, :]).then_inc(swapped.sem, 16)

                    def tanh_gate(k, name):
                        have(name)
                        act.activation(sg[:, k, :], proj[T[name] % 2][:, :], ACT.Tanh, scale=0.5).then_inc(tanh_done.sem, 1)

                    def merge_gate(m):
                        have(f"m{m}")
                        act.wait_ge(*gstored[m % 3].at(G, 16 * (m // 3)))
                        free(act.activation(gstage[:, m % 3, :], proj[T[f"m{m}"] % 2][:, :], ACT.Tanh, scale=0.5))
                        act.wait_ge(*free_of(f"m{m}", L, i))
                        act.dma_start(gate_d[i * 6 + m, :, :], gstage[:, m % 3, :]).then_inc(gstored[m % 3].sem, 16)

                    def exp(j):
                        act.wait_ge(*max_ready.at(G, j + 1))
                        if j >= 4:
                            act.wait_ge(*w_ready.at(G, unit_of(j - 4) + 1))
                        src, k = (score[j % 2][:, :], 1.0) if j < 8 else (sneg[:, j % 2, :], -1.0)
                        act.activation(probs[:, j % 4, :], src, ACT.Exp, bias=negmax[:, j:j + 1], scale=k,
                                       accum_out=sums[:, j:j + 1]).then_inc(exp_done.sem, 1)

                    def turned(u):
                        act.wait_ge(*turn_done.at(G, u + 1))
                        if u == 4:
                            act.wait_ge(*out_done.at(G, 3))
                        if u == 8:
                            act.wait_ge(*pv_done.at(G, 1))
                        q = (u % 4) * P
                        act.activation(wt[:, :, q:q + P], turn[u % 2][:, :].rearrange("p (k q) -> p k q", k=QB),
                                       ACT.Copy).then_inc(wt_ready.sem, 1)

                    tanh_gate(0, "ag")
                    act.wait_ge(*kturn_done.at(G, 1))
                    act.activation(kend[:, :, :], turn[0][:, :].rearrange("p (b c) -> p b c", b=QB), ACT.Copy).then_inc(kend_ready.sem, 1)
                    tanh_gate(1, "bg")
                    tanh_gate(2, "cg")
                    exp(0)
                    exp(1)
                    act.wait_ge(*out_done.at(G, 1))
                    act.activation(sq[:, 0, :], obank[:, :], ACT.Square).then_inc(sq_done.sem, 1)
                    merge_gate(0)
                    for u in range(3):
                        exp(2 * u + 2)
                        exp(2 * u + 3)
                        turned(u)
                        if u == 1:
                            merge_gate(1)
                    exp(8)
                    exp(9)
                    turned(3)
                    merge_gate(2)
                    act.wait_ge(*out_done.at(G, 3))
                    act.activation(sq[:, 1, :], obank[:, :], ACT.Square).then_inc(sq_done.sem, 1)
                    for u in range(4, 10):
                        exp(u + 6)
                        turned(u)
                        if u == 5:
                            merge_gate(3)
                            act.wait_ge(*out_done.at(G, 2))
                            grp.did(act.activation(rr[:, 0, :], mbank[:, :], ACT.Ln, bias=cst[:, 0:1]))
                            have("sumB")
                            free(act.activation(rr[:, 1, :], proj[T["sumB"] % 2][:, :], ACT.Ln, bias=cst[:, 0:1]))
                            act.wait_ge(*free_of("sumB", L, i))
                            act.activation(rr[:, :, :], rr[:, :, :], ACT.Exp, scale=-0.5).then_inc(r_done.sem, 1)
                        if u == 8:
                            merge_gate(4)
                    turned(10)
                    merge_gate(5)
                    turned(11)
                    grp.close()

            mean_square_of_x(DEPTH)
            act.wait_ge(*xsum_done.at(DEPTH, 1))
            act.activation(rx[:, :], proj[0][:, :], ACT.Ln, bias=cst[:, 0:1]).then_inc(act_pre.sem, 1)
            act.wait_ge(*act_pre.at(DEPTH, 1))
            act.activation(rx[:, :], rx[:, :], ACT.Exp, scale=-0.5).then_inc(xr_done.sem, 1)

        @block.vector
        def _(dve):
            dve.sem_inc(y_read.sem, 1)
            dve.sem_inc(z_read.sem, 6)
            dve.sem_inc(x_ready.sem, 8)
            dve.sem_inc(mixed.sem, 2)
            for t, val in ((mean[:, 0, :], 1 / P), (mean[:, 1, :], 1 / D), (cst[:, 0:1], EPS), (cst[:, 1:2], 1.0),
                           (state[:, :, :], 0.0), (att[:, :, :], 0.0)):
                last = dve.memset(t, val)
            last.then_inc(s_init.sem, 1)
            dve.wait_ge(*s_init.at(0, 1))
            dve.wait_ge(*s_const.at(1, 0))
            dve.wait_ge(*s_x.at(0, 16))

            def normed(L, g, done):
                dve.wait_ge(*xr_done.at(L, 1))
                for k in range(KT):
                    dve.scalar_tensor_tensor(h[:, k, :], x[:, k, :], g[:, k:k + 1], rx[:, :], ALU.mult, ALU.mult).then_inc(done.sem, 1)

            with dve.Fori(0, DEPTH) as L:
                chain = Chain(dve, dve_pre, L)
                dve.wait_ge(*s_par.at(L, 16))
                dve.wait_ge(*wt_ready.at(L * NG, 0))
                dl = par[:, C_DL:C_DL + 4 * HD].rearrange("p (n d) -> p n d", n=4)
                chain.did(dve.tensor_tensor_reduce(junk[:, :], dl[:, 0, :], dl[:, 1, :], 1.0, 0.0, ALU.mult, ALU.add, sc[:, 0:1]))
                chain.last()
                chain.did(dve.tensor_tensor_reduce(junk[:, :], dl[:, 2, :], dl[:, 3, :], 1.0, 0.0, ALU.mult, ALU.add, sc[:, 1:2]))
                normed(L, par[:, C_NG:C_NG + KT], h_ready)
                dve.wait_ge(*lam_exp.at(L, 1))
                chain.did(dve.tensor_tensor(sc[:, 2:3], sc[:, 1:2], sc[:, 0:1], ALU.subtract))
                chain.last()
                chain.did(dve.tensor_tensor(sc[:, 2:3], sc[:, 2:3], par[:, C_LI:C_LI + 1], ALU.subtract))
                chain.did(dve.tensor_scalar(sc[:, 3:4], par[:, C_GA:C_GA + 1], 0.5, None, ALU.mult))
                chain.did(dve.tensor_scalar(sc[:, 4:5], par[:, C_GD:C_GD + 1], par[:, C_LI + 1:C_LI + 2], 0.5, ALU.mult, ALU.mult))
                for hd in range(NG):
                    dve.wait_ge(*gate_done.at(L, hd + 1))
                    dve.tensor_scalar(la[:, hd, :], zbanks[hd][:, :], par[:, C_GB + hd:C_GB + hd + 1], 0.0, ALU.add, ALU.min).then_inc(min_done.sem, 1)
                dve.wait_ge(*min_done.at(L, NG))
                dve.wait_ge(*soft_ready.at(L, 1))
                dve.tensor_tensor(la[:, :, :], la[:, :, :], wt[:, :, :], ALU.subtract).then_inc(la_ready.sem, 1)
                dve.wait_ge(*la_ready.at(L, 1))
                apart(dve)
                chain.close()

                with dve.Fori(0, NG) as i:
                    G = L * NG + i
                    grp = Chain(dve, dve_grp, G)
                    dve.wait_ge(*wt_ready.at(G, 0))

                    def have(name):
                        dve.wait_ge(*tile_done.at(L, i * NT + (T[name] + 1)))

                    def free(ins):
                        return ins.then_inc(dve_free.sem, 1)

                    f, b = slice(0, DK), slice(DK, P)
                    grp.did(dve.tensor_copy(rest[:, :], la[:, i, :]))
                    grp.last()
                    grp.did(dve.tensor_tensor_scan(cum[f, :], cmask[f, :], rest[f, :], 0.0, ALU.mult, ALU.add))
                    grp.did(dve.tensor_tensor_scan(cum[b, ::-1], cmask[b, ::-1], rest[b, ::-1], 0.0, ALU.mult, ALU.add))
                    grp.last()
                    cumc = cum[:, :].rearrange("p (n c) -> p n c", n=NC)
                    grp.did(dve.tensor_copy(total[f, :], cumc[f, :, CH - 1]))
                    grp.did(dve.tensor_copy(total[b, :], cumc[b, :, 0]))
                    grp.last()
                    dve.tensor_tensor(rest[:, :].rearrange("p (n c) -> p n c", n=NC),
                                      total[:, :].unsqueeze(2).to_broadcast([P, NC, CH]), cumc, ALU.subtract).then_inc(cum_ready.sem, 1)
                    have("aq")
                    dve.wait_ge(*decay_done.at(G, 4))
                    free(dve.scalar_tensor_tensor(qhat[:, :], proj[T["aq"] % 2][:, :], DK ** -0.5, qhat[:, :], ALU.mult, ALU.mult))
                    have("ak")
                    grp.did(dve.tensor_tensor(cum[:, :], proj[T["ak"] % 2][:, :], cum[:, :], ALU.mult))
                    free(dve.tensor_tensor(rest[:, :], proj[T["ak"] % 2][:, :], rest[:, :], ALU.mult))

                    def rotate(n):
                        dve.wait_ge(*swapped.at(G, 64 * (n + 1)))
                        q, k = 2 * n, 2 * n + 1
                        grp.did(dve.scalar_tensor_tensor(qk[:, q, :], raw[:, 0, :], HD ** -0.5, cos[:, :], ALU.mult, ALU.mult))
                        grp.did(dve.scalar_tensor_tensor(rot[:, 0, :], rot[:, 0, :], HD ** -0.5, sin[:, :], ALU.mult, ALU.mult))
                        grp.did(dve.tensor_tensor(qk[:, k, :], raw[:, 1, :], cos[:, :], ALU.mult))
                        grp.did(dve.tensor_tensor(rot[:, 1, :], rot[:, 1, :], sin[:, :], ALU.mult))
                        grp.last()
                        dve.tensor_tensor(qk[:, q:q + 2, :], qk[:, q:q + 2, :], rot[:, :, :], ALU.add).then_inc(qk_ready.sem, 1)

                    rotate(0)
                    rotate(1)

                    def silu(k, name):
                        dve.wait_ge(*tanh_done.at(G, k + 1))
                        free(dve.scalar_tensor_tensor(sg[:, k, :], sg[:, k, :], 1.0, proj[T[name] % 2][:, :], ALU.add, ALU.mult))

                    silu(0, "ag")
                    dve.wait_ge(*glaatt_done.at(G, 1))
                    apart(dve)
                    for n in range(2):
                        ins = dve.copy_predicated(att[:, n, :].rearrange("p (b c) -> p b c", b=QB),
                                                  gmask[:, n, :].unsqueeze(1).to_broadcast([P, QB, P]),
                                                  score[n][:, :].rearrange("p (b c) -> p b c", b=QB))
                    ins.then_inc(att_ready.sem, 1)
                    silu(1, "bg")
                    dve.wait_ge(*upd_done.at(G, 1))

                    def update(n):
                        return (mbank if n % 2 else turn[1])[:, (n // 2) * DV:(n // 2 + 1) * DV]

                    for n in range(NC - 1):
                        r = NC - 1 - n
                        if n:
                            grp.last()
                        dve.scalar_tensor_tensor(state[f, n + 1, :], state[f, n, :], decay[f, n:n + 1], update(n)[f, :], ALU.mult, ALU.add)
                        ins = dve.scalar_tensor_tensor(state[b, r - 1, :], state[b, r, :], decay[b, r:r + 1], update(r)[b, :], ALU.mult, ALU.add)
                        if n < NC - 2:
                            grp.did(ins)
                    ins.then_inc(state_ready.sem, 1)
                    silu(2, "cg")

                    def row_max(j):
                        dve.wait_ge(*score_done.at(G, j + 1))
                        if j < 8:
                            dve.tensor_reduce(negmax[:, j:j + 1], score[j % 2][:, :], AX_X, ALU.max, negate=True).then_inc(max_ready.sem, 1)
                        else:
                            if j >= 10:
                                dve.wait_ge(*exp_done.at(G, j - 1))
                            apart(dve)
                            dve.tensor_tensor_reduce(sneg[:, j % 2, :], score[j % 2][:, :], lmask[:, j % 4, :], -1.0, 3.0e38,
                                                     ALU.add, ALU.min, negmax[:, j:j + 1]).then_inc(max_ready.sem, 1)

                    def weights(u):
                        if u >= 2:
                            dve.wait_ge(*turn_done.at(G, u - 1))
                        if u < 4:
                            a, c = 2 * u, 2 * u + 1
                            dve.wait_ge(*exp_done.at(G, c + 1))
                            grp.did(dve.reciprocal(rs[:, a:a + 2], sums[:, a:a + 2]))
                            grp.last()
                            grp.did(dve.tensor_tensor(rs[:, c:c + 1], rs[:, c:c + 1], sc[:, 2:3], ALU.mult))
                            grp.did(dve.tensor_scalar(w[:, u % 2, :], probs[:, a % 4, :], rs[:, a:a + 1], None, ALU.mult))
                            grp.last()
                            dve.scalar_tensor_tensor(w[:, u % 2, :], probs[:, c % 4, :], rs[:, c:c + 1], w[:, u % 2, :],
                                                     ALU.mult, ALU.add).then_inc(w_ready.sem, 1)
                        else:
                            j = u + 4
                            dve.wait_ge(*exp_done.at(G, j + 1))
                            grp.did(dve.reciprocal(rs[:, j:j + 1], sums[:, j:j + 1]))
                            grp.last()
                            dve.tensor_scalar(w[:, u % 2, :], probs[:, j % 4, :], rs[:, j:j + 1], None, ALU.mult).then_inc(w_ready.sem, 1)

                    row_max(0)
                    row_max(1)
                    dve.wait_ge(*sq_done.at(G, 1))
                    dve.scalar_tensor_tensor(y[:, i, :], obank[:, :], sc[:, 3:4], sg[:, 0, :], ALU.mult, ALU.mult).then_inc(y_read.sem, 1)
                    for u in range(4):
                        row_max(2 * u + 2)
                        row_max(2 * u + 3)
                        weights(u)
                    row_max(10)
                    weights(4)
                    dve.wait_ge(*sq_done.at(G, 2))
                    dve.scalar_tensor_tensor(y[:, NG + i, :], obank[:, :], sc[:, 4:5], sg[:, 1, :], ALU.mult, ALU.mult).then_inc(y_read.sem, 1)
                    for u in range(5, 12):
                        if u < 10:
                            row_max(u + 6)
                        weights(u)
                        if u == 8:
                            dve.wait_ge(*r_done.at(G, 1))
                            dve.wait_ge(*y_read.at(G, 2))
                            grp.did(dve.tensor_tensor(y[:, i, :], y[:, i, :], rr[:, 0, :], ALU.mult))
                            grp.did(dve.tensor_tensor(y[:, NG + i, :], y[:, NG + i, :], rr[:, 1, :], ALU.mult))
                    dve.wait_ge(*out_done.at(G, 4))
                    dve.scalar_tensor_tensor(y[:, 2 * NG + i, :], mbank[:, :], 0.5, sg[:, 2, :], ALU.mult, ALU.mult).then_inc(y_read.sem, 1)
                    dve.wait_ge(*y_read.at(G, 3))
                    grp.close()

                mix = Chain(dve, dve_mix, L)
                for d in range(KT):
                    dve.wait_ge(*gloaded[d % 2].at(L, 16 * (d // 2 + 1)))
                    for g in range(3):
                        zt = 3 * d + g
                        dve.wait_ge(*tile_done.at(L, NG * NT + zt + 1))
                        if g == 0 and d:
                            dve.wait_ge(*mixed.at(L, d))
                        dst = za[:, 0, :] if g == 0 else za[:, 1, :]
                        if g == 2:
                            mix.last()
                        dve.scalar_tensor_tensor(dst, gates[:, d % 2, g, :], 1.0, zbanks[zt % 6][:, :], ALU.add, ALU.mult).then_inc(z_read.sem, 1)
                        if g == 1:
                            dve.wait_ge(*z_read.at(L, zt + 1))
                            mix.did(dve.tensor_tensor(za[:, 0, :], za[:, 0, :], za[:, 1, :], ALU.add))
                    dve.wait_ge(*z_read.at(L, 3 * d + 3))
                    dve.tensor_tensor(h[:, d, :], za[:, 0, :], za[:, 1, :], ALU.add).then_inc(mixed.sem, 1)
                for e in range(KT):
                    dve.wait_ge(*tile_done.at(L, NG * NT + 24 + e + 1))
                    dve.scalar_tensor_tensor(x[:, e, :], proj[e % 2][:, :], 0.5, x[:, e, :], ALU.mult, ALU.add).then_inc(x_ready.sem, 1)
                dve.wait_ge(*x_ready.at(L + 1, 0))
                mix.close()

            normed(DEPTH, fin, out_ready)

        @block.tensor
        def _(pe):
            pe.sem_inc(tile_done.sem, LAYER_TILES)
            pe.wait_ge(*s_init.at(0, 1))
            pe.wait_ge(*s_const.at(1, 0))

            def x_mean(L):
                for k in range(KT):
                    if k % 2 == 0:
                        pe.wait_ge(*xsq_done.at(L, k // 2 + 1))
                    last = pe.matmul(proj[0][:, :], mean[:, 1, :], h[:, k, :], start=(k == 0), stop=(k == KT - 1))
                last.then_inc(xsum_done.sem, 1)

            with pe.Fori(0, DEPTH) as L:
                x_mean(L)
                pe.wait_ge(*s_par.at(L, 16))
                for k in range(KT):
                    pe.wait_ge(*h_ready.at(L, k + 1))
                    last = pe.matmul(proj[1][0:2 * RANK, :], par[:, C_LOW + 32 * k:C_LOW + 32 * k + 32], h[:, k, :],
                                     start=(k == 0), stop=(k == KT - 1))
                last.then_inc(low_done.sem, 1)
                pe.wait_ge(*low_ready.at(L, 1))
                for hd in range(NG):
                    pe.matmul(zbanks[hd][:, :], par[0:2 * RANK, C_UP + P * hd:C_UP + P * hd + P], low[:, :],
                              start=True, stop=True).then_inc(gate_done.sem, 1)

                with pe.Fori(0, NG) as i:
                    G = L * NG + i

                    def arrived(u):
                        s = u % RING
                        pe.wait_ge(*loaded[s].at(L, 16 * (i * 3 + (u // RING + 1))))

                    def bank_free(t):
                        if t >= 2:
                            pe.wait_ge(*free_of(TILES[t - 2], L, i))
                        elif t == 0:
                            pe.wait_ge(*act_free.at(L, len(BY_ACT) * i))

                    def project(name):
                        t, u = T[name], 3 + UNIT_TILES.index(name)
                        arrived(u)
                        bank_free(t)
                        for k in range(KT):
                            last = pe.matmul(proj[t % 2][:, :], ring[:, u % RING, k, :], h[:, k, :], start=(k == 0), stop=(k == KT - 1))
                        last.then_inc(tile_done.sem, 1)

                    for u in range(3):
                        arrived(u)
                    for b in range(QB):
                        bank_free(b)
                        for k in range(KT):
                            last = pe.matmul(proj[b % 2][:, 0:3 * P], h[:, k, P * b:P * b + P], ring[:, 0:3, k, :],
                                             start=(k == 0), stop=(k == KT - 1))
                        last.then_inc(tile_done.sem, 1)
                    for name in ("aq", "ak", "bq", "bk", "cq", "ck", "ag"):
                        project(name)

                    pe.wait_ge(*free_of("ak", L, i))
                    for n in range(2):
                        r = slice(DK * n, DK * n + DK)
                        for b in range(QB):
                            t = slice(P * b, P * b + P)
                            last = pe.matmul(score[n][:, t], cum[r, t], qhat[r, t], start=(b == 0), stop=(b == QB - 1), skip_group_check=True)
                    last.then_inc(glaatt_done.sem, 1)
                    for b in range(QB):
                        last = pe.transpose(turn[0][:, P * b:P * b + P], rest[:, P * b:P * b + P], ident[:, :])
                    last.then_inc(kturn_done.sem, 1)
                    project("bg")
                    pe.wait_ge(*kend_ready.at(G, 1))
                    for n in range(NC):
                        r = slice(CH * (n % 2), CH * (n % 2) + CH)
                        dst = (mbank if n % 2 else turn[1])[:, (n // 2) * DV:(n // 2 + 1) * DV]
                        last = pe.matmul(dst, kend[r, n // 2, :], v[r, n // 2, 0:DV], start=(n < 2), stop=(n >= NC - 2), skip_group_check=True)
                    last.then_inc(upd_done.sem, 1)
                    project("cg")

                    def scores(j):
                        if j == 0:
                            pe.wait_ge(*qk_ready.at(G, 2))
                            pe.wait_ge(*att_ready.at(G, 1))
                        if 2 <= j < 10:
                            pe.wait_ge(*exp_done.at(G, j - 1))
                        elif j >= 10:
                            pe.wait_ge(*max_ready.at(G, j - 1))
                        if j < 8:
                            q, r, b = 0, slice(HD * (j % 2), HD * (j % 2) + HD), j // 2
                        else:
                            q, r, b = 2, slice(HD * ((j - 8) // 4), HD * ((j - 8) // 4) + HD), j % 4
                        pe.matmul(score[j % 2][:, :], qk[r, q, P * b:P * b + P], qk[r, q + 1, :], start=True, stop=True).then_inc(score_done.sem, 1)

                    def turn_weights(u):
                        pe.wait_ge(*w_ready.at(G, u + 1))
                        if u >= 2:
                            pe.wait_ge(*wt_ready.at(G, u - 1))
                        for k in range(QB):
                            last = pe.transpose(turn[u % 2][:, P * k:P * k + P], w[:, u % 2, P * k:P * k + P], ident[:, :])
                        last.then_inc(turn_done.sem, 1)

                    def values(dst, cols, ready, done):
                        pe.wait_ge(*wt_ready.at(G, ready))
                        for k in range(QB):
                            last = pe.matmul(dst, v[:, k, cols], wt[:, k, :], start=(k == 0), stop=(k == QB - 1))
                        last.then_inc(done.sem, 1)

                    scores(0)
                    scores(1)
                    pe.wait_ge(*state_ready.at(G, 1))
                    first = True
                    for b in range(QB):
                        for n in range(2):
                            t = slice(P * b, P * b + P)
                            pe.matmul(obank[:, t], v[:, b, 0:DV], att[:, n, t], start=first, stop=False, skip_group_check=True)
                            first = False
                        for n in (2 * b, 2 * b + 1):
                            t = slice(CH * n, CH * n + CH)
                            last = pe.matmul(obank[:, t], state[:, n, :], qhat[:, t], start=False, stop=(n == NC - 1), skip_group_check=True)
                    last.then_inc(out_done.sem, 1)
                    project("m0")
                    pe.wait_ge(*sq_done.at(G, 1))
                    pe.matmul(mbank[:, :], mean[:, 0, :], sq[:, 0, :], start=True, stop=True).then_inc(out_done.sem, 1)
                    for u in range(3):
                        scores(2 * u + 2)
                        scores(2 * u + 3)
                        turn_weights(u)
                        if u == 1:
                            project("m1")
                    scores(8)
                    scores(9)
                    turn_weights(3)
                    project("m2")
                    pe.wait_ge(*y_read.at(G, 1))
                    values(obank[:, :], slice(P, 2 * P), 4, out_done)
                    for u in range(4, 10):
                        scores(u + 6)
                        turn_weights(u)
                        if u == 5:
                            project("m3")
                            pe.wait_ge(*sq_done.at(G, 2))
                            bank_free(T["sumB"])
                            pe.matmul(proj[T["sumB"] % 2][:, :], mean[:, 0, :], sq[:, 1, :], start=True, stop=True).then_inc(tile_done.sem, 1)
                        if u == 7:
                            pe.wait_ge(*r_done.at(G, 1))
                            values(mbank[0:HD, :], slice(2 * P, 2 * P + HD), 8, pv_done)
                        if u == 8:
                            project("m4")
                    turn_weights(10)
                    project("m5")
                    turn_weights(11)
                    values(mbank[HD:P, :], slice(2 * P + HD, 3 * P), 12, out_done)

                pe.wait_ge(*y_read.at(L * NG + NG, 0))
                apart(pe)
                with pe.Fori(0, 2) as half:
                    for zt in range(12):
                        c = zt // 2
                        if zt % 2 == 0:
                            pe.wait_ge(*loaded[c].at(L, 16 * (half + 13)))
                        pe.wait_ge(*z_read.at(L, half * 12 + (zt - 5)))
                        for k in range(NG):
                            n = 4 * zt + k
                            last = pe.matmul(zbanks[zt % 6][:, :], ring[:, n // 8, n % 8, :], y[:, NG * (zt % 3) + k, :],
                                             start=(k == 0), stop=(k == NG - 1))
                        last.then_inc(tile_done.sem, 1)
                pe.wait_ge(*mixed.at(L, 8))
                pe.wait_ge(*act_free.at(L + 1, 0))
                apart(pe)
                with pe.Fori(0, 2) as half:
                    for e in range(4):
                        pe.wait_ge(*loaded[e].at(L, 16 * (half + 15)))
                        pe.wait_ge(*x_ready.at(L, half * 4 + (e - 1)))
                        for k in range(KT):
                            last = pe.matmul(proj[e % 2][:, :], ring[:, e, k, :], h[:, k, :], start=(k == 0), stop=(k == KT - 1))
                        last.then_inc(tile_done.sem, 1)
            x_mean(DEPTH)


def tables():
    half = HD // 2
    inv = (1.0 / THETA ** (np.arange(0, HD, 2, dtype=np.float32) / HD)).astype(np.float32)
    ang = np.arange(S, dtype=np.float32)[:, None] * inv[None, :]
    lane = np.arange(P) % half
    sign = np.where(np.arange(P) % HD < half, -1.0, 1.0).astype(np.float32)
    cos = np.cos(ang)[:, lane].T
    sin = np.sin(ang)[:, lane].T * sign[:, None]
    i, j = np.arange(S)[:, None], np.arange(S)[None, :]
    count = np.zeros((S, S), np.int64)
    for window, dil in PATTERNS:
        count += ((i - j) % dil == 0) & (np.abs(i - j) // dil <= window // (2 * dil))
    logs = np.where(count > 0, np.log(np.maximum(count, 1)), -1e30).astype(np.float32)
    lmask = logs.reshape(QB, P, S).transpose(1, 0, 2)
    t = np.arange(S) % CH
    cmask = np.ones((P, S), np.float32)
    cmask[:DK, t == 0] = 0
    cmask[DK:, t == CH - 1] = 0
    a, b = np.arange(P)[:, None], np.arange(P)[None, :]
    same = a // CH == b // CH
    gmask = np.stack([same & (a <= b), same & (a >= b)], 1).astype(np.uint32)
    return [np.ascontiguousarray(t) for t in (cos.astype(np.float32), sin.astype(np.float32), lmask, cmask, gmask,
                                              np.eye(P, dtype=np.float32))]


def columns():
    names = ["aq", "ak", "av", "ag", "lf", "lb", "bq", "bk", "bv", "bg", "cq", "ck", "cv", "cg", "m"]
    widths = [256, 256, 512, 512, 16, 16] + [512] * 8 + [3072]
    starts = np.cumsum([0] + widths[:-1])
    return dict(zip(names, starts.tolist()))


def stream(w_in, w_branch, w_out):
    at = columns()
    w_in = w_in.reshape(DEPTH, KT, P, -1)
    order = []
    for i in range(NG):
        for name in ("av", "bv", "cv"):
            order.append(np.arange(P) + at[name] + P * i)
        for name in UNIT_TILES:
            if name in ("aq", "ak"):
                order.append(np.arange(P) % DK + at[name] + DK * i)
            elif name[0] == "m":
                n = 6 * i + int(name[1])
                order.append(np.arange(P) + at["m"] + (n % 3) * D + (n // 3) * P)
            else:
                order.append(np.arange(P) + at[name] + P * i)
    out = np.empty((DEPTH, ROWS_LAYER, P, 8, P), np.float32)
    for u, cols in enumerate(order):
        out[:, u] = w_in[:, :, :, cols].transpose(0, 2, 1, 3)
    wb = w_branch.reshape(DEPTH, 3, NG, P, KT, P).transpose(0, 4, 1, 2, 3, 5).reshape(DEPTH, 12, 8, P, P)
    out[:, NG * GU:NG * GU + 12] = wb.transpose(0, 1, 3, 2, 4)
    out[:, NG * GU + 12:] = w_out.reshape(DEPTH, KT, P, KT, P).transpose(0, 3, 2, 1, 4)
    return out.reshape(DEPTH * ROWS_LAYER, P, 8 * P)


def parameters(w_in, norm_g, gate_up, gate_b, gla_g, diff_lambda, diff_g):
    out = np.zeros((DEPTH, P, NPAR), np.float32)
    lo = columns()["lf"]
    out[:, :, C_LOW:C_UP] = w_in[:, :, lo:lo + 2 * RANK].reshape(DEPTH, KT, P, 2 * RANK).transpose(0, 2, 1, 3).reshape(DEPTH, P, -1)
    for hd in range(NG):
        for d in range(2):
            c = C_UP + P * hd + DK * d
            out[:, RANK * d:RANK * d + RANK, c:c + DK] = gate_up[:, d, :, DK * hd:DK * hd + DK]
            out[:, DK * d:DK * d + DK, C_GB + hd] = gate_b[:, d, DK * hd:DK * hd + DK]
    out[:, :, C_NG:C_NG + KT] = norm_g.reshape(DEPTH, KT, P).transpose(0, 2, 1)
    out[:, :, C_GA] = gla_g
    out[:, :, C_GD] = diff_g
    out[:, :, C_DL:C_DL + 4 * HD] = diff_lambda.reshape(DEPTH, 1, -1)
    for layer in range(DEPTH):
        init = 0.8 - 0.6 * math.exp(-0.3 * layer)
        out[layer, :, C_LI] = init
        out[layer, :, C_LI + 1] = 1.0 - init
    return out


def kernel(x, norm_g, w_in, gla_gate_up, gla_gate_b, gla_norm_g, diff_lambda, diff_norm_g, w_branch, w_out, final_norm_g):
    import concourse.bacc as bacc
    from concourse.bass_utils import run_bass_kernel_spmd as run

    x, norm_g, w_in, gla_gate_up, gla_gate_b, gla_norm_g, diff_lambda, diff_norm_g, w_branch, w_out, final_norm_g = (
        np.asarray(a) for a in (x, norm_g, w_in, gla_gate_up, gla_gate_b, gla_norm_g, diff_lambda, diff_norm_g, w_branch,
                                w_out, final_norm_g))
    cos, sin, lmask, cmask, gmask, ident = tables()
    arrays = {
        "x_t": np.ascontiguousarray(x.reshape(S, KT, P).transpose(2, 1, 0)),
        "weights": stream(w_in, w_branch, w_out),
        "params": parameters(w_in, norm_g, gla_gate_up, gla_gate_b, gla_norm_g, diff_lambda, diff_norm_g),
        "final_g": np.ascontiguousarray(final_norm_g.reshape(KT, P).T),
        "cos_t": cos, "sin_t": sin, "lmask_t": lmask, "cmask_t": cmask, "gmask_t": gmask, "ident_t": ident,
    }
    nc = bacc.Bacc("TRN2", target_bir_lowering=False, num_devices=1)
    args = [nc.dram_tensor(n, a.shape, mybir.dt.from_np(a.dtype), kind="ExternalInput").ap() for n, a in arrays.items()]
    out = nc.dram_tensor("out_t", (P, KT, S), F32, kind="ExternalOutput").ap()
    gate_scratch = nc.dram_tensor("gate_scratch", (3 * KT, P, S), F32, kind="Internal").ap()
    build(nc, *args, out, gate_scratch)
    r = run(nc, [arrays], core_ids=[0])
    return np.ascontiguousarray(r.results[0]["out_t"].transpose(2, 1, 0)).reshape(1, S, D)
```

```python
import math
from contextlib import ExitStack

import numpy as np

import concourse.bass as bass
from concourse import mybir

F32 = mybir.dt.float32
F32R = mybir.dt.float32r
U32 = mybir.dt.uint32
ACT = mybir.ActivationFunctionType
ALU = mybir.AluOpType
AX_X = mybir.AxisListType.X

P = 128
DEPTH, S, D = 2, 512, 1024
KT = D // P
QB = S // P
NG = 4
BW = 512
DK, DV = 64, 128
RANK = 16
CH = 64
NC = S // CH
HD = 64
THETA, EPS = 10000.0, 1e-6
PATTERNS = ((128, 1), (512, 4), (2048, 16))
TAU = 16.0

TILES = ["v0", "v1", "v2", "v3", "aq", "ak", "bq", "bk", "cq", "ck", "ag", "bg", "cg",
         "m0", "m1", "m2", "sumB", "m3", "m4", "m5"]
NT = len(TILES)
T = {name: n for n, name in enumerate(TILES)}
UNIT_TILES = [n for n in TILES[4:] if n != "sumB"]
GU = 3 + len(UNIT_TILES)
ROWS_LAYER = 1 + NG * GU + 12 + 8
BRANCH_ROW, OUT_ROW = 1 + NG * GU, 1 + NG * GU + 12
RAW = 3
assert ROWS_LAYER % RAW == 0
SLOT = [0, 1, 2, 3, 0, 1, 2, 3, 0, 1, 2, 3, 1, 2, 0, 1, 2, 3]
SPLIT = 4
LAYER_TILES = 1 + NG * NT + 24 + 8
BRANCH_TILE, OUT_TILE = 1 + NG * NT, 1 + NG * NT + 24
LAYER_SPLITS = 1 + NG * GU + 8
BY_DVE = ["aq", "ak", "ag", "bg", "cg"]
BY_ACT = [n for n in TILES if n not in BY_DVE]

C_NG, C_GA, C_GD, C_DL, C_LI, NPAR = 0, 8, 9, 10, 266, 268


class Signal:

    def __init__(self, sem, per, credit=0):
        self.sem, self.per, self.credit = sem, per, credit

    def at(self, n, k):
        return self.sem, n * self.per + (self.credit + k)


class Chain:

    def __init__(self, eng, steps, n):
        self.eng, self.steps, self.n, self.k = eng, steps, n, 0

    def did(self, ins):
        ins.then_inc(self.steps.sem, 1)
        self.k += 1
        return self.k

    def need(self, k):
        self.eng.wait_ge(*self.steps.at(self.n, k))

    def last(self):
        self.need(self.k)

    def close(self):
        assert self.k == self.steps.per, (self.k, self.steps.per)


def freed_by(u):
    return 4 if u < 3 else T[UNIT_TILES[u - 3]] + 1


def unit_of(j):
    return j // 2 if j < 8 else j - 4


def build(nc, x_d, w_d, par_d, up_d, fin_d, cos_d, sin_d, lmask_d, cmask_d, gmask_d, ident_d, out_d, gate_d, xkeep_d):
    with ExitStack() as ctx:
        def sb(name, shape, dt=F32):
            return ctx.enter_context(nc.sbuf_tensor(name, shape, dt))

        def bank(name):
            return ctx.enter_context(nc.psum_tensor(name, [P, S], F32))

        def sig(name, per, credit=0):
            return Signal(ctx.enter_context(nc.semaphore(name)), per, credit)

        big = sb("big", [P, KT, S])
        x, qk, wt = big, big[:, 0:4, :], big[:, 4:8, :]
        hh = sb("hh", [P, KT, S], F32R)
        hl = sb("hl", [P, KT, S], F32R)
        y = sb("y", [P, 3 * NG, S])
        raw_w = sb("raw_w", [P, RAW, 8, P])
        wh = sb("wh", [P, SPLIT, 8, P], F32R)
        wl = sb("wl", [P, SPLIT, 8, P], F32R)
        par = sb("par", [P, NPAR])
        up = sb("up", [P, P + 1])
        sc = sb("sc", [P, 8])
        junk = sb("junk", [P, HD])
        v = sb("v", [P, QB, 3 * P])
        raw = sb("raw", [P, 2, S])
        za = raw
        rot = sb("rot", [P, 2, S])
        low = sb("low", [2 * RANK, S])
        cum = sb("cum", [P, S])
        rest = sb("rest", [P, S])
        qhat = sb("qhat", [P, S])
        sqa, sqb = rest, cum
        total = sb("total", [P, NC])
        decay = sb("decay", [P, NC])
        kend = sb("kend", [P, QB, P])
        att = sb("att", [P, 2, S])
        state = sb("state", [P, NC, DV])
        sg = sb("sg", [P, 3, S])
        six = sb("six", [P, 6, S])
        probs, sneg = six[:, 0:4, :], six[:, 4:6, :]
        gates = six[:, :, :].rearrange("p (n g) s -> p n g s", n=2)
        w = sb("w", [P, 2, S])
        rr = sb("rr", [P, 2, S])
        rx = rr[:, 0, :]
        negmax = sb("negmax", [P, 16])
        sums = sb("sums", [P, 16])
        rs = sb("rs", [P, 16])
        gstage = sb("gstage", [P, 2, S])
        cos = sb("cos", [P, S])
        sin = sb("sin", [P, S])
        lmask = sb("lmask", [P, QB, S])
        cmask = sb("cmask", [P, S])
        gmask = sb("gmask", [P, 2, P], U32)
        ident = sb("ident", [P, P])
        mean = sb("mean", [P, 2, P])
        cst = sb("cst", [P, 2])
        fin = sb("fin", [P, KT])

        proj = [bank("proj0"), bank("proj1")]
        score = [bank("score0"), bank("score1")]
        turn = [bank("turn0"), bank("turn1")]
        obank, mbank = bank("obank"), bank("mbank")
        zbanks = score + turn + [obank, mbank]

        s_x = [sig(f"s_x{n}", 16) for n in range(4)]
        s_const = sig("s_const", 16 * 7)
        s_par = sig("s_par", 16)
        s_up = sig("s_up", 16)
        loaded = [sig(f"loaded{s}", 16 * ROWS_LAYER // RAW) for s in range(RAW)]
        s_init = sig("s_init", 0)
        s_passed = sig("s_passed", 0)
        tile_done = sig("tile_done", LAYER_TILES, LAYER_TILES)
        xsum_done = sig("xsum_done", KT)
        gate_done = sig("gate_done", 1)
        glaatt_done = sig("glaatt_done", 1)
        kturn_done = sig("kturn_done", 1)
        upd_done = sig("upd_done", 1)
        score_done = sig("score_done", 16)
        turn_done = sig("turn_done", 12)
        pv_done = sig("pv_done", 1)
        out_done = sig("out_done", 4)
        act_free = sig("act_free", len(BY_ACT) * NG, 1)
        xsq_done = sig("xsq_done", KT)
        xr_done = sig("xr_done", 1)
        act_pre = sig("act_pre", 1)
        hh_ready = sig("hh_ready", KT)
        low_ready = sig("low_ready", 1)
        soft_ready = sig("soft_ready", 1, 1)
        lam_exp = sig("lam_exp", 1)
        decay_done = sig("decay_done", 4)
        tanh_done = sig("tanh_done", 3)
        kend_ready = sig("kend_ready", 1)
        exp_done = sig("exp_done", 16)
        wt_ready = sig("wt_ready", 12, 1)
        sq_done = sig("sq_done", 2)
        r_done = sig("r_done", 1)
        act_grp = sig("act_grp", 3)
        dve_free = sig("dve_free", len(BY_DVE) * NG)
        dve_pre = sig("dve_pre", 6)
        min_done = sig("min_done", 1)
        t_ready = sig("t_ready", KT)
        h_ready = sig("h_ready", KT)
        cum_ready = sig("cum_ready", 1)
        qk_ready = sig("qk_ready", 2)
        att_ready = sig("att_ready", 1)
        state_ready = sig("state_ready", 1)
        max_ready = sig("max_ready", 16)
        w_ready = sig("w_ready", 12)
        y_read = sig("y_read", 3, 1)
        dve_grp = sig("dve_grp", 42)
        z_read = sig("z_read", 24, 6)
        mixed = sig("mixed", 8, 2)
        dve_mix = sig("dve_mix", 24)
        x_ready = sig("x_ready", 8, 8)
        out_ready = sig("out_ready", 8)
        split_done = sig("split_done", LAYER_SPLITS, RAW)
        pool_high = sig("pool_high", LAYER_SPLITS)
        swapped = sig("swapped", 2 * 64)
        gstored = [sig(f"gstored{s}", 3 * 16, 16) for s in range(2)]
        x_kept = sig("x_kept", 16)
        x_back = sig("x_back", 16)
        gloaded = [sig(f"gloaded{s}", 4 * 16) for s in range(2)]
        s_out = sig("s_out", 16)

        block = ctx.enter_context(nc.Block())

        def free_of(name, L, i):
            if name in BY_DVE:
                return dve_free.at(L, len(BY_DVE) * i + (BY_DVE.index(name) + 1))
            return act_free.at(L, len(BY_ACT) * i + (BY_ACT.index(name) + 1))

        def apart(eng):
            eng.sem_inc(s_passed.sem, 1)

        @block.sync
        def _(sp):
            for n in range(4):
                t = slice(2 * n, 2 * n + 2)
                sp.dma_start(x[:, t, :], x_d[:, t, :]).then_inc(s_x[n].sem, 16)

            def unit(L, row, slot):
                sp.dma_start(raw_w[:, slot, :, :], w_d[L * ROWS_LAYER + row, :, :].rearrange(
                    "p (t c) -> p t c", c=P)).then_inc(loaded[slot].sem, 16)

            with sp.Fori(0, DEPTH) as L:
                sp.wait_ge(*y_read.at(L * NG, 0))
                sp.dma_start(par[:, :], par_d[L, :, :]).then_inc(s_par.sem, 16)
                for n in range(RAW + 1):
                    sp.wait_ge(*split_done.at(L, n + 1 - RAW))
                    unit(L, n, n % RAW)
                sp.wait_ge(*x_ready.at(L, 0))
                for n in range(4):
                    sp.wait_ge(*s_x[n].at(0, 16))
                sp.dma_start(xkeep_d, x[:, :, :]).then_inc(x_kept.sem, 16)
                with sp.Fori(0, NG) as i:
                    sp.wait_ge(*soft_ready.at(L * NG + i, 0))
                    sp.dma_start(up[:, :], up_d[L * NG + i, :, :]).then_inc(s_up.sem, 16)
                    for j in range(GU):
                        sp.wait_ge(*split_done.at(L, i * GU + (j + 2)))
                        unit(L, i * GU + (RAW + 1 + j), (RAW + 1 + j) % RAW)
                for c in range(RAW, 12):
                    sp.wait_ge(*tile_done.at(L, BRANCH_TILE + 2 * (c - RAW + 1)))
                    unit(L, BRANCH_ROW + c, (BRANCH_ROW + c) % RAW)
                    if c == 8:
                        sp.wait_ge(*x_kept.at(L + 1, 0))
                        sp.dma_start(x[:, :, :], xkeep_d).then_inc(x_back.sem, 16)
                for o in range(8):
                    if o < RAW:
                        sp.wait_ge(*tile_done.at(L, BRANCH_TILE + 2 * (12 - RAW + o + 1)))
                    else:
                        sp.wait_ge(*split_done.at(L, 1 + NG * GU + (o - RAW + 1)))
                    unit(L, OUT_ROW + o, (OUT_ROW + o) % RAW)
            for k in range(KT):
                sp.wait_ge(*out_ready.at(0, k + 1))
                sp.dma_start(out_d[:, k, :], y[:, k, :]).then_inc(s_out.sem, 16)
            sp.wait_ge(*s_out.at(0, 16 * KT))

        @block.gpsimd
        def _(pool):
            pool.sem_inc(split_done.sem, RAW)
            pool.wait_ge(*s_x[3].at(0, 16))
            for dst, src in ((cos[:, :], cos_d), (sin[:, :], sin_d), (lmask[:, :, :], lmask_d), (cmask[:, :], cmask_d),
                             (gmask[:, :, :], gmask_d), (ident[:, :], ident_d), (fin[:, :], fin_d)):
                pool.dma_start(dst, src).then_inc(s_const.sem, 16)

            def split(L, n, row, slot, free):
                src = raw_w[:, ROW0(row) % RAW, :, :]
                pool.wait_ge(*loaded[ROW0(row) % RAW].at(L, 16 * (row_uses(row))))
                pool.wait_ge(*tile_done.at(L, free))
                apart(pool)
                pool.tensor_scalar(wh[:, slot, :, :], src, 1.0, 1.0, ALU.mult, ALU.mult).then_inc(pool_high.sem, 1)
                pool.wait_ge(*pool_high.at(L, n + 1))
                apart(pool)
                pool.tensor_tensor(wl[:, slot, :, :], src, wh[:, slot, :, :].bitcast(F32), ALU.subtract).then_inc(split_done.sem, 1)

            def ROW0(row):
                return row[1]

            def row_uses(row):
                i, c = row
                return i * (GU // RAW) + (c // RAW + 1)

            with pool.Fori(0, DEPTH) as L:
                split(L, 0, (0, 0), 3, OUT_TILE + 8 - LAYER_TILES)
                for u in range(3):
                    split(L, 1 + u, (0, 1 + u), SLOT[u], OUT_TILE + 5 + u - LAYER_TILES)

                def tiles(i):
                    for u in range(3, GU):
                        before = [t for t in range(u) if SLOT[t] == SLOT[u]]
                        split(L, i * GU + (1 + u), (i, 1 + u), SLOT[u], i * NT + (1 + (freed_by(before[-1]) if before else 0)))

                with pool.Fori(0, NG - 1) as i:
                    tiles(i)
                    for u in range(3):
                        last = max(t for t in range(GU) if SLOT[t] == SLOT[u])
                        split(L, i * GU + (1 + GU + u), (i, 1 + GU + u), SLOT[u], i * NT + (1 + freed_by(last)))
                tiles(NG - 1)
                for s in range(2):
                    pool.wait_ge(*gstored[s].at((L + 1) * NG, 0))
                pool.wait_ge(*y_read.at((L + 1) * NG, 0))
                for d in range(KT):
                    pool.wait_ge(*mixed.at(L, d - 1))
                    apart(pool)
                    pool.dma_start(gates[:, d % 2, :, :], gate_d[3 * d:3 * d + 3, :, :].rearrange(
                        "g p s -> p g s")).then_inc(gloaded[d % 2].sem, 16)
                for s in range(2):
                    pool.wait_ge(*gloaded[s].at(L + 1, 0))
                for o in range(8):
                    last = BRANCH_TILE if o < SPLIT else OUT_TILE + o - SPLIT + 1
                    split(L, 1 + NG * GU + o, (0, OUT_ROW + o), o % SPLIT, last)

        @block.scalar
        def _(act):
            act.sem_inc(act_free.sem, 1)
            act.sem_inc(wt_ready.sem, 1)
            act.sem_inc(soft_ready.sem, 1)
            for s in range(2):
                act.sem_inc(gstored[s].sem, 16)
            act.wait_ge(*s_init.at(0, 1))

            def square_of_x(n, e):
                act.wait_ge(*x_ready.at(n - 1, e + 1))
                if e >= 6:
                    act.wait_ge(*xsum_done.at(n, e - 5))
                act.activation(six[:, e % 6, :], x[:, e, :], ACT.Square).then_inc(xsq_done.sem, 1)

            def rsqrt_of_x(n):
                act.wait_ge(*xsum_done.at(n, KT))
                act.activation(rx, mbank[:, :], ACT.Ln, bias=cst[:, 0:1]).then_inc(act_pre.sem, 1)
                act.wait_ge(*act_pre.at(n, 1))
                act.activation(rx, rx, ACT.Exp, scale=-0.5).then_inc(xr_done.sem, 1)

            for e in range(KT):
                act.wait_ge(*s_x[e // 2].at(0, 16))
                square_of_x(0, e)
            with act.Fori(0, DEPTH) as L:
                rsqrt_of_x(L)
                act.wait_ge(*dve_pre.at(L, 2))
                act.activation(sc[:, 0:2], sc[:, 0:2], ACT.Exp).then_inc(lam_exp.sem, 1)
                for k in range(KT):
                    act.wait_ge(*t_ready.at(L, k + 1))
                    act.activation(hh[:, k, :], six[:, k % 6, :], ACT.Copy).then_inc(hh_ready.sem, 1)
                act.wait_ge(*tile_done.at(L, 1))
                act.activation(low[:, :], proj[1][0:2 * RANK, :], ACT.Copy).then_inc(low_ready.sem, 1)

                with act.Fori(0, NG) as i:
                    G = L * NG + i
                    grp = Chain(act, act_grp, G)

                    def have(name):
                        act.wait_ge(*tile_done.at(L, i * NT + (T[name] + 2)))

                    def free(ins):
                        return ins.then_inc(act_free.sem, 1)

                    act.wait_ge(*min_done.at(G, 1))
                    grp.did(act.activation(qhat[:, :], turn[0][:, :], ACT.Abs, bias=up[:, P:P + 1]))
                    grp.last()
                    grp.did(act.activation(qhat[:, :], qhat[:, :], ACT.Exp, scale=-1.0))
                    grp.last()
                    act.activation(qhat[:, :], qhat[:, :], ACT.Ln, bias=cst[:, 1:2]).then_inc(soft_ready.sem, 1)
                    act.wait_ge(*cum_ready.at(G, 1))
                    act.activation(qhat[:, :], cum[:, :], ACT.Exp, scale=1 / TAU).then_inc(decay_done.sem, 1)
                    act.activation(rest[:, :], rest[:, :], ACT.Exp, scale=1 / TAU).then_inc(decay_done.sem, 1)
                    act.activation(decay[:, :], total[:, :], ACT.Exp, scale=1 / TAU).then_inc(decay_done.sem, 1)
                    act.wait_ge(*decay_done.at(G, 1))
                    act.activation(cum[:, :], cum[:, :], ACT.Exp, scale=-1 / TAU).then_inc(decay_done.sem, 1)
                    for b in range(QB):
                        have(f"v{b}")
                        free(act.activation(v[:, b, :], proj[b % 2][:, 0:3 * P], ACT.Copy))
                    for n, (q, k) in enumerate((("bq", "bk"), ("cq", "ck"))):
                        for m, name in enumerate((q, k)):
                            have(name)
                            if n:
                                act.wait_ge(*qk_ready.at(G, 1))
                            free(act.activation(raw[:, m, :], proj[T[name] % 2][:, :], ACT.Copy))
                        act.wait_ge(*free_of(k, L, i))
                        for a in range(4):
                            b = a ^ 1
                            act.dma_start(rot[32 * a:32 * a + 32, :, :], raw[32 * b:32 * b + 32, :, :]).then_inc(swapped.sem, 16)

                    def tanh_gate(k, name):
                        have(name)
                        act.activation(sg[:, k, :], proj[T[name] % 2][:, :], ACT.Tanh, scale=0.5).then_inc(tanh_done.sem, 1)

                    def merge_gate(m):
                        have(f"m{m}")
                        act.wait_ge(*gstored[m % 2].at(G, 16 * (m // 2)))
                        free(act.activation(gstage[:, m % 2, :], proj[T[f"m{m}"] % 2][:, :], ACT.Tanh, scale=0.5))
                        act.wait_ge(*free_of(f"m{m}", L, i))
                        act.dma_start(gate_d[i * 6 + m, :, :], gstage[:, m % 2, :]).then_inc(gstored[m % 2].sem, 16)

                    def exp(j):
                        act.wait_ge(*max_ready.at(G, j + 1))
                        if j >= 4:
                            act.wait_ge(*w_ready.at(G, unit_of(j - 4) + 1))
                        src, k = (score[j % 2][:, :], 1.0) if j < 8 else (sneg[:, j % 2, :], -1.0)
                        act.activation(probs[:, j % 4, :], src, ACT.Exp, bias=negmax[:, j:j + 1], scale=k,
                                       accum_out=sums[:, j:j + 1]).then_inc(exp_done.sem, 1)

                    def turned(u):
                        act.wait_ge(*turn_done.at(G, u + 1))
                        if u == 4:
                            act.wait_ge(*out_done.at(G, 3))
                        if u == 8:
                            act.wait_ge(*pv_done.at(G, 1))
                        q = (u % 4) * P
                        act.activation(wt[:, :, q:q + P], turn[u % 2][:, :].rearrange("p (k q) -> p k q", k=QB),
                                       ACT.Copy).then_inc(wt_ready.sem, 1)

                    act.wait_ge(*kturn_done.at(G, 1))
                    act.activation(kend[:, :, :], turn[0][:, :].rearrange("p (b c) -> p b c", b=QB), ACT.Copy).then_inc(kend_ready.sem, 1)
                    tanh_gate(0, "ag")
                    tanh_gate(1, "bg")
                    exp(0)
                    exp(1)
                    act.wait_ge(*out_done.at(G, 1))
                    act.activation(sqa[:, :], obank[:, :], ACT.Square).then_inc(sq_done.sem, 1)
                    for u in range(4):
                        exp(2 * u + 2)
                        exp(2 * u + 3)
                        turned(u)
                        if u == 0:
                            tanh_gate(2, "cg")
                        if u >= 2:
                            merge_gate(u - 2)
                    act.wait_ge(*out_done.at(G, 3))
                    act.activation(sqb[:, :], obank[:, :], ACT.Square).then_inc(sq_done.sem, 1)
                    for u in range(4, 10):
                        exp(u + 6)
                        turned(u)
                        if u == 5:
                            merge_gate(2)
                            act.wait_ge(*out_done.at(G, 2))
                            grp.did(act.activation(rr[:, 0, :], mbank[:, :], ACT.Ln, bias=cst[:, 0:1]))
                            have("sumB")
                            free(act.activation(rr[:, 1, :], proj[T["sumB"] % 2][:, :], ACT.Ln, bias=cst[:, 0:1]))
                            act.wait_ge(*free_of("sumB", L, i))
                            act.activation(rr[:, :, :], rr[:, :, :], ACT.Exp, scale=-0.5).then_inc(r_done.sem, 1)
                        if u == 7:
                            merge_gate(3)
                        if u == 9:
                            merge_gate(4)
                    turned(10)
                    turned(11)
                    merge_gate(5)
                    grp.close()

                for e in range(KT):
                    square_of_x(L + 1, e)

            rsqrt_of_x(DEPTH)

        @block.vector
        def _(dve):
            dve.sem_inc(y_read.sem, 1)
            dve.sem_inc(z_read.sem, 6)
            dve.sem_inc(x_ready.sem, 8)
            dve.sem_inc(mixed.sem, 2)
            for t, val in ((mean[:, 0, :], 1 / P), (mean[:, 1, :], 1 / D), (cst[:, 0:1], EPS), (cst[:, 1:2], 1.0),
                           (state[:, :, :], 0.0), (att[:, :, :], 0.0)):
                last = dve.memset(t, val)
            last.then_inc(s_init.sem, 1)
            dve.wait_ge(*s_init.at(0, 1))
            dve.wait_ge(*s_const.at(1, 0))
            for n in range(4):
                dve.wait_ge(*s_x[n].at(0, 16))

            def normed(L, k, dst, g):
                return dve.scalar_tensor_tensor(dst, x[:, k, :], g[:, k:k + 1], rx, ALU.mult, ALU.mult)

            with dve.Fori(0, DEPTH) as L:
                chain = Chain(dve, dve_pre, L)
                dve.wait_ge(*s_par.at(L, 16))
                dl = par[:, C_DL:C_DL + 4 * HD].rearrange("p (n d) -> p n d", n=4)
                apart(dve)
                chain.did(dve.tensor_tensor_reduce(junk[:, :], dl[:, 0, :], dl[:, 1, :], 1.0, 0.0, ALU.mult, ALU.add, sc[:, 0:1]))
                chain.last()
                apart(dve)
                chain.did(dve.tensor_tensor_reduce(junk[:, :], dl[:, 2, :], dl[:, 3, :], 1.0, 0.0, ALU.mult, ALU.add, sc[:, 1:2]))
                dve.wait_ge(*xr_done.at(L, 1))

                def low_part(k):
                    dve.wait_ge(*hh_ready.at(L, k + 1))
                    dve.tensor_tensor(hl[:, k, :], six[:, k % 6, :], hh[:, k, :].bitcast(F32), ALU.subtract).then_inc(h_ready.sem, 1)

                for k in range(KT):
                    if k >= 6:
                        dve.wait_ge(*h_ready.at(L, k - 5))
                    normed(L, k, six[:, k % 6, :], par[:, C_NG:C_NG + KT]).then_inc(t_ready.sem, 1)
                    if k:
                        low_part(k - 1)
                low_part(KT - 1)
                dve.wait_ge(*lam_exp.at(L, 1))
                chain.did(dve.tensor_tensor(sc[:, 2:3], sc[:, 1:2], sc[:, 0:1], ALU.subtract))
                chain.last()
                chain.did(dve.tensor_tensor(sc[:, 2:3], sc[:, 2:3], par[:, C_LI:C_LI + 1], ALU.subtract))
                chain.did(dve.tensor_scalar(sc[:, 3:4], par[:, C_GA:C_GA + 1], 0.5, None, ALU.mult))
                chain.did(dve.tensor_scalar(sc[:, 4:5], par[:, C_GD:C_GD + 1], par[:, C_LI + 1:C_LI + 2], 0.5, ALU.mult, ALU.mult))
                chain.last()
                chain.close()
                apart(dve)

                with dve.Fori(0, NG) as i:
                    G = L * NG + i
                    grp = Chain(dve, dve_grp, G)
                    dve.wait_ge(*wt_ready.at(G, 0))

                    def have(name):
                        dve.wait_ge(*tile_done.at(L, i * NT + (T[name] + 2)))

                    def free(ins):
                        return ins.then_inc(dve_free.sem, 1)

                    dve.wait_ge(*gate_done.at(G, 1))
                    dve.tensor_scalar(rest[:, :], turn[0][:, :], up[:, P:P + 1], 0.0, ALU.add, ALU.min).then_inc(min_done.sem, 1)
                    dve.wait_ge(*soft_ready.at(G, 1))
                    grp.did(dve.tensor_tensor(rest[:, :], rest[:, :], qhat[:, :], ALU.subtract))
                    grp.last()
                    f, b = slice(0, DK), slice(DK, P)
                    grp.did(dve.tensor_tensor_scan(cum[f, :], cmask[f, :], rest[f, :], 0.0, ALU.mult, ALU.add))
                    grp.did(dve.tensor_tensor_scan(cum[b, ::-1], cmask[b, ::-1], rest[b, ::-1], 0.0, ALU.mult, ALU.add))
                    grp.last()
                    cumc = cum[:, :].rearrange("p (n c) -> p n c", n=NC)
                    grp.did(dve.tensor_copy(total[f, :], cumc[f, :, CH - 1]))
                    grp.did(dve.tensor_copy(total[b, :], cumc[b, :, 0]))
                    grp.last()
                    dve.tensor_tensor(rest[:, :].rearrange("p (n c) -> p n c", n=NC),
                                      total[:, :].unsqueeze(2).to_broadcast([P, NC, CH]), cumc, ALU.subtract).then_inc(cum_ready.sem, 1)
                    have("aq")
                    dve.wait_ge(*decay_done.at(G, 4))
                    free(dve.scalar_tensor_tensor(qhat[:, :], proj[T["aq"] % 2][:, :], DK ** -0.5, qhat[:, :], ALU.mult, ALU.mult))
                    have("ak")
                    grp.did(dve.tensor_tensor(cum[:, :], proj[T["ak"] % 2][:, :], cum[:, :], ALU.mult))
                    free(dve.tensor_tensor(rest[:, :], proj[T["ak"] % 2][:, :], rest[:, :], ALU.mult))

                    def rotate(n):
                        dve.wait_ge(*swapped.at(G, 64 * (n + 1)))
                        q, k = 2 * n, 2 * n + 1
                        grp.did(dve.scalar_tensor_tensor(qk[:, q, :], raw[:, 0, :], HD ** -0.5, cos[:, :], ALU.mult, ALU.mult))
                        grp.did(dve.scalar_tensor_tensor(rot[:, 0, :], rot[:, 0, :], HD ** -0.5, sin[:, :], ALU.mult, ALU.mult))
                        grp.did(dve.tensor_tensor(qk[:, k, :], raw[:, 1, :], cos[:, :], ALU.mult))
                        grp.did(dve.tensor_tensor(rot[:, 1, :], rot[:, 1, :], sin[:, :], ALU.mult))
                        grp.last()
                        dve.tensor_tensor(qk[:, q:q + 2, :], qk[:, q:q + 2, :], rot[:, :, :], ALU.add).then_inc(qk_ready.sem, 1)

                    dve.wait_ge(*x_kept.at(L, 16))
                    rotate(0)
                    rotate(1)

                    def silu(k, name):
                        dve.wait_ge(*tanh_done.at(G, k + 1))
                        free(dve.scalar_tensor_tensor(sg[:, k, :], sg[:, k, :], 1.0, proj[T[name] % 2][:, :], ALU.add, ALU.mult))

                    silu(0, "ag")
                    dve.wait_ge(*glaatt_done.at(G, 1))
                    apart(dve)
                    for n in range(2):
                        ins = dve.copy_predicated(att[:, n, :].rearrange("p (b c) -> p b c", b=QB),
                                                  gmask[:, n, :].unsqueeze(1).to_broadcast([P, QB, P]),
                                                  score[n][:, :].rearrange("p (b c) -> p b c", b=QB))
                    ins.then_inc(att_ready.sem, 1)
                    dve.wait_ge(*upd_done.at(G, 1))

                    def update(n):
                        return (mbank if n % 2 else turn[1])[:, (n // 2) * DV:(n // 2 + 1) * DV]

                    for n in range(NC - 1):
                        r = NC - 1 - n
                        if n:
                            grp.last()
                        dve.scalar_tensor_tensor(state[f, n + 1, :], state[f, n, :], decay[f, n:n + 1], update(n)[f, :], ALU.mult, ALU.add)
                        ins = dve.scalar_tensor_tensor(state[b, r - 1, :], state[b, r, :], decay[b, r:r + 1], update(r)[b, :], ALU.mult, ALU.add)
                        if n < NC - 2:
                            grp.did(ins)
                    ins.then_inc(state_ready.sem, 1)
                    silu(1, "bg")

                    def row_max(j):
                        dve.wait_ge(*score_done.at(G, j + 1))
                        if j < 8:
                            dve.tensor_reduce(negmax[:, j:j + 1], score[j % 2][:, :], AX_X, ALU.max, negate=True).then_inc(max_ready.sem, 1)
                        else:
                            if j >= 10:
                                dve.wait_ge(*exp_done.at(G, j - 1))
                            apart(dve)
                            dve.tensor_tensor_reduce(sneg[:, j % 2, :], score[j % 2][:, :], lmask[:, j % 4, :], -1.0, 3.0e38,
                                                     ALU.add, ALU.min, negmax[:, j:j + 1]).then_inc(max_ready.sem, 1)

                    def weights(u):
                        if u >= 2:
                            dve.wait_ge(*turn_done.at(G, u - 1))
                        if u < 4:
                            a, c = 2 * u, 2 * u + 1
                            dve.wait_ge(*exp_done.at(G, c + 1))
                            grp.did(dve.reciprocal(rs[:, a:a + 2], sums[:, a:a + 2]))
                            grp.last()
                            grp.did(dve.tensor_tensor(rs[:, c:c + 1], rs[:, c:c + 1], sc[:, 2:3], ALU.mult))
                            grp.did(dve.tensor_scalar(w[:, u % 2, :], probs[:, a % 4, :], rs[:, a:a + 1], None, ALU.mult))
                            grp.last()
                            dve.scalar_tensor_tensor(w[:, u % 2, :], probs[:, c % 4, :], rs[:, c:c + 1], w[:, u % 2, :],
                                                     ALU.mult, ALU.add).then_inc(w_ready.sem, 1)
                        else:
                            j = u + 4
                            dve.wait_ge(*exp_done.at(G, j + 1))
                            grp.did(dve.reciprocal(rs[:, j:j + 1], sums[:, j:j + 1]))
                            grp.last()
                            dve.tensor_scalar(w[:, u % 2, :], probs[:, j % 4, :], rs[:, j:j + 1], None, ALU.mult).then_inc(w_ready.sem, 1)

                    row_max(0)
                    row_max(1)
                    dve.wait_ge(*sq_done.at(G, 1))
                    dve.scalar_tensor_tensor(y[:, i, :], obank[:, :], sc[:, 3:4], sg[:, 0, :], ALU.mult, ALU.mult).then_inc(y_read.sem, 1)
                    for u in range(4):
                        row_max(2 * u + 2)
                        row_max(2 * u + 3)
                        weights(u)
                        if u == 1:
                            silu(2, "cg")
                    row_max(10)
                    weights(4)
                    dve.wait_ge(*sq_done.at(G, 2))
                    dve.scalar_tensor_tensor(y[:, NG + i, :], obank[:, :], sc[:, 4:5], sg[:, 1, :], ALU.mult, ALU.mult).then_inc(y_read.sem, 1)
                    for u in range(5, 12):
                        if u < 10:
                            row_max(u + 6)
                        weights(u)
                        if u == 8:
                            dve.wait_ge(*r_done.at(G, 1))
                            dve.wait_ge(*y_read.at(G, 2))
                            grp.did(dve.tensor_tensor(y[:, i, :], y[:, i, :], rr[:, 0, :], ALU.mult))
                            grp.did(dve.tensor_tensor(y[:, NG + i, :], y[:, NG + i, :], rr[:, 1, :], ALU.mult))
                    dve.wait_ge(*out_done.at(G, 4))
                    dve.scalar_tensor_tensor(y[:, 2 * NG + i, :], mbank[:, :], 0.5, sg[:, 2, :], ALU.mult, ALU.mult).then_inc(y_read.sem, 1)
                    dve.wait_ge(*y_read.at(G, 3))
                    grp.close()

                mix = Chain(dve, dve_mix, L)
                for d in range(KT):
                    dve.wait_ge(*gloaded[d % 2].at(L, 16 * (d // 2 + 1)))
                    for g in range(3):
                        zt = 3 * d + g
                        dve.wait_ge(*tile_done.at(L, BRANCH_TILE + zt + 1))
                        if g == 0 and d:
                            dve.wait_ge(*mixed.at(L, d))
                        dst = za[:, 0, :] if g == 0 else za[:, 1, :]
                        if g == 2:
                            mix.last()
                        dve.scalar_tensor_tensor(dst, gates[:, d % 2, g, :], 1.0, zbanks[zt % 6][:, :], ALU.add, ALU.mult).then_inc(z_read.sem, 1)
                        if g == 1:
                            dve.wait_ge(*z_read.at(L, zt + 1))
                            mix.did(dve.tensor_tensor(za[:, 0, :], za[:, 0, :], za[:, 1, :], ALU.add))
                    dve.wait_ge(*z_read.at(L, 3 * d + 3))
                    mix.did(dve.tensor_tensor(hh[:, d, :], za[:, 0, :], za[:, 1, :], ALU.add))
                    mix.did(dve.tensor_tensor(za[:, 0, :], za[:, 0, :], za[:, 1, :], ALU.add))
                    mix.last()
                    dve.tensor_tensor(hl[:, d, :], za[:, 0, :], hh[:, d, :].bitcast(F32), ALU.subtract).then_inc(mixed.sem, 1)
                mix.close()
                dve.wait_ge(*x_back.at(L, 16))
                for e in range(KT):
                    dve.wait_ge(*tile_done.at(L, OUT_TILE + e + 1))
                    dve.scalar_tensor_tensor(x[:, e, :], proj[e % 2][:, :], 0.5, x[:, e, :], ALU.mult, ALU.add).then_inc(x_ready.sem, 1)
                dve.wait_ge(*x_ready.at(L + 1, 0))
                apart(dve)

            dve.wait_ge(*xr_done.at(DEPTH, 1))
            for k in range(KT):
                normed(DEPTH, k, y[:, k, :], fin).then_inc(out_ready.sem, 1)

        @block.tensor
        def _(pe):
            pe.sem_inc(tile_done.sem, LAYER_TILES)
            pe.wait_ge(*s_init.at(0, 1))

            def x_mean(n, e):
                pe.wait_ge(*xsq_done.at(n, e + 1))
                pe.matmul(mbank[:, :], mean[:, 1, :], six[:, e % 6, :], start=(e == 0), stop=(e == KT - 1)).then_inc(xsum_done.sem, 1)

            def product(dst, slot, ks):
                for k in ks:
                    for a, b in ((wh, hh), (wh, hl), (wl, hh)):
                        last = pe.matmul(dst, a[:, slot, k, :], b[:, k, :], start=(k == 0 and a is wh and b is hh),
                                         stop=(k == KT - 1 and a is wl))
                return last

            for e in range(KT):
                x_mean(0, e)
            pe.wait_ge(*s_const.at(1, 0))
            with pe.Fori(0, DEPTH) as L:
                pe.wait_ge(*split_done.at(L, 1))
                for k in range(KT):
                    pe.wait_ge(*h_ready.at(L, k + 1))
                    last = product(proj[1][:, :], 3, [k])
                last.then_inc(tile_done.sem, 1)
                pe.wait_ge(*low_ready.at(L, 1))
                apart(pe)

                with pe.Fori(0, NG) as i:
                    G = L * NG + i

                    def arrived(u):
                        pe.wait_ge(*split_done.at(L, i * GU + (u + 2)))

                    def bank_free(t):
                        if t >= 2:
                            pe.wait_ge(*free_of(TILES[t - 2], L, i))
                        elif t == 0:
                            pe.wait_ge(*act_free.at(L, len(BY_ACT) * i))

                    def project(name, half=None):
                        t, u = T[name], 3 + UNIT_TILES.index(name)
                        if not half:
                            arrived(u)
                            bank_free(t)
                        ks = range(KT) if half is None else range(4 * half, 4 * half + 4)
                        last = product(proj[t % 2][:, :], SLOT[u], ks)
                        if half != 0:
                            last.then_inc(tile_done.sem, 1)

                    pe.wait_ge(*s_up.at(G, 16))
                    pe.matmul(turn[0][:, :], up[0:2 * RANK, 0:P], low[:, :], start=True, stop=True).then_inc(gate_done.sem, 1)
                    arrived(2)
                    for b in range(QB):
                        bank_free(b)
                        for k in range(KT):
                            for n, (a, c) in enumerate(((hh, wh), (hh, wl), (hl, wh))):
                                last = pe.matmul(proj[b % 2][:, 0:3 * P], a[:, k, P * b:P * b + P], c[:, 0:3, k, :],
                                                 start=(k == 0 and n == 0), stop=(k == KT - 1 and n == 2))
                        last.then_inc(tile_done.sem, 1)
                    for name in ("aq", "ak", "bq", "bk", "cq", "ck"):
                        project(name)

                    pe.wait_ge(*free_of("ak", L, i))
                    for n in range(2):
                        r = slice(DK * n, DK * n + DK)
                        for b in range(QB):
                            t = slice(P * b, P * b + P)
                            last = pe.matmul(score[n][:, t], cum[r, t], qhat[r, t], start=(b == 0), stop=(b == QB - 1), skip_group_check=True)
                    last.then_inc(glaatt_done.sem, 1)
                    for b in range(QB):
                        last = pe.transpose(turn[0][:, P * b:P * b + P], rest[:, P * b:P * b + P], ident[:, :])
                    last.then_inc(kturn_done.sem, 1)
                    project("ag")
                    pe.wait_ge(*kend_ready.at(G, 1))
                    for n in range(NC):
                        r = slice(CH * (n % 2), CH * (n % 2) + CH)
                        dst = (mbank if n % 2 else turn[1])[:, (n // 2) * DV:(n // 2 + 1) * DV]
                        last = pe.matmul(dst, kend[r, n // 2, :], v[r, n // 2, 0:DV], start=(n < 2), stop=(n >= NC - 2), skip_group_check=True)
                    last.then_inc(upd_done.sem, 1)
                    project("bg")

                    def scores(j):
                        if j == 0:
                            pe.wait_ge(*qk_ready.at(G, 2))
                            pe.wait_ge(*att_ready.at(G, 1))
                        if 2 <= j < 10:
                            pe.wait_ge(*exp_done.at(G, j - 1))
                        elif j >= 10:
                            pe.wait_ge(*max_ready.at(G, j - 1))
                        if j < 8:
                            q, r, b = 0, slice(HD * (j % 2), HD * (j % 2) + HD), j // 2
                        else:
                            q, r, b = 2, slice(HD * ((j - 8) // 4), HD * ((j - 8) // 4) + HD), j % 4
                        pe.matmul(score[j % 2][:, :], qk[r, q, P * b:P * b + P], qk[r, q + 1, :], start=True, stop=True).then_inc(score_done.sem, 1)

                    def turn_weights(u):
                        pe.wait_ge(*w_ready.at(G, u + 1))
                        if u >= 2:
                            pe.wait_ge(*wt_ready.at(G, u - 1))
                        for k in range(QB):
                            last = pe.transpose(turn[u % 2][:, P * k:P * k + P], w[:, u % 2, P * k:P * k + P], ident[:, :])
                        last.then_inc(turn_done.sem, 1)

                    def values(dst, cols, ready, done):
                        pe.wait_ge(*wt_ready.at(G, ready))
                        for k in range(QB):
                            last = pe.matmul(dst, v[:, k, cols], wt[:, k, :], start=(k == 0), stop=(k == QB - 1))
                        last.then_inc(done.sem, 1)

                    scores(0)
                    scores(1)
                    pe.wait_ge(*state_ready.at(G, 1))
                    first = True
                    for b in range(QB):
                        for n in range(2):
                            t = slice(P * b, P * b + P)
                            pe.matmul(obank[:, t], v[:, b, 0:DV], att[:, n, t], start=first, stop=False, skip_group_check=True)
                            first = False
                        for n in (2 * b, 2 * b + 1):
                            t = slice(CH * n, CH * n + CH)
                            last = pe.matmul(obank[:, t], state[:, n, :], qhat[:, t], start=False, stop=(n == NC - 1), skip_group_check=True)
                    last.then_inc(out_done.sem, 1)
                    project("cg", 0)
                    pe.wait_ge(*sq_done.at(G, 1))
                    pe.matmul(mbank[:, :], mean[:, 0, :], sqa[:, :], start=True, stop=True).then_inc(out_done.sem, 1)
                    fill = [(name, n) for name in ("cg", "m0", "m1", "m2", "m3", "m4", "m5") for n in range(2)][1:]
                    for u in range(4):
                        scores(2 * u + 2)
                        scores(2 * u + 3)
                        project(*fill.pop(0))
                        turn_weights(u)
                    project(*fill.pop(0))
                    values(obank[:, :], slice(P, 2 * P), 4, out_done)
                    for u in range(4, 10):
                        scores(u + 6)
                        project(*fill.pop(0))
                        if u == 8:
                            pe.wait_ge(*r_done.at(G, 1))
                            values(mbank[0:HD, :], slice(2 * P, 2 * P + HD), 8, pv_done)
                        turn_weights(u)
                        if u == 5:
                            pe.wait_ge(*sq_done.at(G, 2))
                            bank_free(T["sumB"])
                            pe.matmul(proj[T["sumB"] % 2][:, :], mean[:, 0, :], sqb[:, :], start=True, stop=True).then_inc(tile_done.sem, 1)
                    project(*fill.pop(0))
                    turn_weights(10)
                    turn_weights(11)
                    project(*fill.pop(0))
                    values(mbank[HD:P, :], slice(2 * P + HD, 3 * P), 12, out_done)

                pe.wait_ge(*y_read.at(L * NG + NG, 0))
                apart(pe)
                with pe.Fori(0, 2) as half:
                    for zt in range(12):
                        c = BRANCH_ROW + zt // 2
                        if zt % 2 == 0:
                            pe.wait_ge(*loaded[c % RAW].at(L, 16 * (half * (6 // RAW) + (c // RAW + 1))))
                        pe.wait_ge(*z_read.at(L, half * 12 + (zt - 5)))
                        for k in range(NG):
                            n = 4 * zt + k
                            last = pe.matmul(zbanks[zt % 6][:, :], raw_w[:, c % RAW, n % 8, :], y[:, NG * (zt % 3) + k, :],
                                             start=(k == 0), stop=(k == NG - 1))
                        last.then_inc(tile_done.sem, 1)
                pe.wait_ge(*act_free.at(L + 1, 0))
                for e in range(2):
                    pe.wait_ge(*split_done.at(L, 1 + NG * GU + (e + 1)))
                    for k in range(KT - 1):
                        if e == 0:
                            pe.wait_ge(*mixed.at(L, k + 1))
                        product(proj[e][:, :], e, [k])
                pe.wait_ge(*mixed.at(L, KT))
                for e in range(KT):
                    if e >= 2:
                        pe.wait_ge(*split_done.at(L, 1 + NG * GU + (e + 1)))
                        pe.wait_ge(*x_ready.at(L, e - 1))
                    product(proj[e % 2][:, :], e % SPLIT, range(KT) if e >= 2 else [KT - 1]).then_inc(tile_done.sem, 1)
                    if e >= 2:
                        x_mean(L + 1, e - 2)
                x_mean(L + 1, KT - 2)
                x_mean(L + 1, KT - 1)


def tables():
    half = HD // 2
    inv = (1.0 / THETA ** (np.arange(0, HD, 2, dtype=np.float32) / HD)).astype(np.float32)
    ang = np.arange(S, dtype=np.float32)[:, None] * inv[None, :]
    lane = np.arange(P) % half
    sign = np.where(np.arange(P) % HD < half, -1.0, 1.0).astype(np.float32)
    cos = np.cos(ang)[:, lane].T
    sin = np.sin(ang)[:, lane].T * sign[:, None]
    i, j = np.arange(S)[:, None], np.arange(S)[None, :]
    count = np.zeros((S, S), np.int64)
    for window, dil in PATTERNS:
        count += ((i - j) % dil == 0) & (np.abs(i - j) // dil <= window // (2 * dil))
    logs = np.where(count > 0, np.log(np.maximum(count, 1)), -1e30).astype(np.float32)
    lmask = logs.reshape(QB, P, S).transpose(1, 0, 2)
    t = np.arange(S) % CH
    cmask = np.ones((P, S), np.float32)
    cmask[:DK, t == 0] = 0
    cmask[DK:, t == CH - 1] = 0
    a, b = np.arange(P)[:, None], np.arange(P)[None, :]
    same = a // CH == b // CH
    gmask = np.stack([same & (a <= b), same & (a >= b)], 1).astype(np.uint32)
    return [np.ascontiguousarray(t) for t in (cos.astype(np.float32), sin.astype(np.float32), lmask, cmask, gmask,
                                              np.eye(P, dtype=np.float32))]


def columns():
    names = ["aq", "ak", "av", "ag", "lf", "lb", "bq", "bk", "bv", "bg", "cq", "ck", "cv", "cg", "m"]
    widths = [256, 256, 512, 512, 16, 16] + [512] * 8 + [3072]
    starts = np.cumsum([0] + widths[:-1])
    return dict(zip(names, starts.tolist()))


def stream(w_in, w_branch, w_out):
    at = columns()
    w_in = w_in.reshape(DEPTH, KT, P, -1)
    order = []
    for i in range(NG):
        for name in ("av", "bv", "cv"):
            order.append(np.arange(P) + at[name] + P * i)
        for name in UNIT_TILES:
            if name in ("aq", "ak"):
                order.append(np.arange(P) % DK + at[name] + DK * i)
            elif name[0] == "m":
                n = 6 * i + int(name[1])
                order.append(np.arange(P) + at["m"] + (n % 3) * D + (n // 3) * P)
            else:
                order.append(np.arange(P) + at[name] + P * i)
    out = np.empty((DEPTH, ROWS_LAYER, P, 8, P), np.float32)
    for i in range(NG):
        for u, cols in enumerate(order[GU * i:GU * i + GU]):
            out[:, 1 + GU * i + u] = w_in[:, :, :, cols].transpose(0, 2, 1, 3)
    out[:, 0] = 0
    out[:, 0, :, :, :2 * RANK] = w_in[:, :, :, at["lf"]:at["lf"] + 2 * RANK].transpose(0, 2, 1, 3)
    wb = w_branch.reshape(DEPTH, 3, NG, P, KT, P).transpose(0, 4, 1, 2, 3, 5).reshape(DEPTH, 12, 8, P, P)
    out[:, BRANCH_ROW:OUT_ROW] = wb.transpose(0, 1, 3, 2, 4)
    out[:, OUT_ROW:] = w_out.reshape(DEPTH, KT, P, KT, P).transpose(0, 3, 2, 1, 4)
    return out.reshape(DEPTH * ROWS_LAYER, P, 8 * P)


def decay_projections(gate_up, gate_b):
    out = np.zeros((DEPTH, NG, P, P + 1), np.float32)
    for hd in range(NG):
        for d in range(2):
            c = DK * d
            out[:, hd, RANK * d:RANK * d + RANK, c:c + DK] = gate_up[:, d, :, DK * hd:DK * hd + DK]
            out[:, hd, c:c + DK, P] = gate_b[:, d, DK * hd:DK * hd + DK]
    return out.reshape(DEPTH * NG, P, P + 1)


def parameters(norm_g, gla_g, diff_lambda, diff_g):
    out = np.zeros((DEPTH, P, NPAR), np.float32)
    out[:, :, C_NG:C_NG + KT] = norm_g.reshape(DEPTH, KT, P).transpose(0, 2, 1)
    out[:, :, C_GA] = gla_g
    out[:, :, C_GD] = diff_g
    out[:, :, C_DL:C_DL + 4 * HD] = diff_lambda.reshape(DEPTH, 1, -1)
    for layer in range(DEPTH):
        init = 0.8 - 0.6 * math.exp(-0.3 * layer)
        out[layer, :, C_LI] = init
        out[layer, :, C_LI + 1] = 1.0 - init
    return out


def kernel(x, norm_g, w_in, gla_gate_up, gla_gate_b, gla_norm_g, diff_lambda, diff_norm_g, w_branch, w_out, final_norm_g):
    import concourse.bacc as bacc
    from concourse.bass_utils import run_bass_kernel_spmd as run

    x, norm_g, w_in, gla_gate_up, gla_gate_b, gla_norm_g, diff_lambda, diff_norm_g, w_branch, w_out, final_norm_g = (
        np.asarray(a) for a in (x, norm_g, w_in, gla_gate_up, gla_gate_b, gla_norm_g, diff_lambda, diff_norm_g, w_branch,
                                w_out, final_norm_g))
    cos, sin, lmask, cmask, gmask, ident = tables()
    arrays = {
        "x_t": np.ascontiguousarray(x.reshape(S, KT, P).transpose(2, 1, 0)),
        "weights": stream(w_in, w_branch, w_out),
        "params": parameters(norm_g, gla_norm_g, diff_lambda, diff_norm_g),
        "decay_w": decay_projections(gla_gate_up, gla_gate_b),
        "final_g": np.ascontiguousarray(final_norm_g.reshape(KT, P).T),
        "cos_t": cos, "sin_t": sin, "lmask_t": lmask, "cmask_t": cmask, "gmask_t": gmask, "ident_t": ident,
    }
    nc = bacc.Bacc("TRN2", target_bir_lowering=False, num_devices=1)
    args = [nc.dram_tensor(n, a.shape, mybir.dt.from_np(a.dtype), kind="ExternalInput").ap() for n, a in arrays.items()]
    out = nc.dram_tensor("out_t", (P, KT, S), F32, kind="ExternalOutput").ap()
    gate_scratch = nc.dram_tensor("gate_scratch", (3 * KT, P, S), F32, kind="Internal").ap()
    x_scratch = nc.dram_tensor("x_scratch", (P, KT, S), F32, kind="Internal").ap()
    build(nc, *args, out, gate_scratch, x_scratch)
    r = run(nc, [arrays], core_ids=[0])
    return np.ascontiguousarray(r.results[0]["out_t"].transpose(2, 1, 0)).reshape(1, S, D)
```

```python
import math
from contextlib import ExitStack

import numpy as np

import concourse.bass as bass
from concourse import mybir

F32 = mybir.dt.float32
F32R = mybir.dt.float32r
U32 = mybir.dt.uint32
ACT = mybir.ActivationFunctionType
ALU = mybir.AluOpType
AX_X = mybir.AxisListType.X

P = 128
DEPTH, S, D = 2, 512, 1024
KT = D // P
QB = S // P
NG = 4
DK, DV = 64, 128
RANK = 16
CH = 64
NC = S // CH
HD = 64
THETA, EPS = 10000.0, 1e-6
PATTERNS = ((128, 1), (512, 4), (2048, 16))
TAU = 16.0

TILES = ["v0", "v1", "v2", "v3", "a", "bq", "bk", "cq", "ck", "ag", "bg", "cg", "m0", "m1", "m2", "m3", "m4", "m5"]
NT = len(TILES)
T = {name: n for n, name in enumerate(TILES)}
UNIT_TILES = TILES[4:]
GU = 3 + len(UNIT_TILES)
ROWS_LAYER = 1 + NG * GU + 12 + 8
BRANCH_ROW, OUT_ROW = 1 + NG * GU, 1 + NG * GU + 12
RAW = 3
LOADS_FIRST = [len([n for n in range(4) if (n + 1) % RAW == s]) for s in range(RAW)]
LOADS_GROUP = [len(range(s, GU, RAW)) for s in range(RAW)]
LOADS_LAYER = [LOADS_FIRST[s] + NG * LOADS_GROUP[s] + len([c for c in range(3, 20) if (c + 2) % RAW == s]) for s in range(RAW)]
assert sum(LOADS_LAYER) == ROWS_LAYER
SLOT = [1, 2, 0, 3, 0, 1, 2, 3, 0, 1, 2, 3, 0, 1, 2, 0, 3]
VALUES = ["bv", "cv", "av"]
assert len(SLOT) == GU and (GU - 3) % RAW == 2
SPLIT = 4
OUT_SLOT = [3, 1, 2, 0]
BRANCH_SLOTS = 3
LAYER_TILES = 1 + NG * NT + 24 + 8
BRANCH_TILE, OUT_TILE = 1 + NG * NT, 1 + NG * NT + 24
FILLERS = ["cg", "m0", "m1", "m2", "m3", "m4", "m5"]
BY_DVE = ["ag", "bg", "cg"]
BY_ACT = [n for n in TILES if n not in BY_DVE]

C_NG, C_GA, C_GD, C_DL, C_LI, NPAR = 0, 8, 9, 10, 266, 268


class Signal:

    def __init__(self, sem, per, credit=0):
        self.sem, self.per, self.credit = sem, per, credit

    def at(self, n, k):
        return self.sem, n * self.per + (self.credit + k)


class Chain:

    def __init__(self, eng, steps, n):
        self.eng, self.steps, self.n, self.k = eng, steps, n, 0

    def did(self, ins):
        ins.then_inc(self.steps.sem, 1)
        self.k += 1
        return self.k

    def need(self, k):
        self.eng.wait_ge(*self.steps.at(self.n, k))

    def last(self):
        self.need(self.k)

    def close(self):
        assert self.k == self.steps.per, (self.k, self.steps.per)


def arrival(n):
    if n < 4:
        return (n + 1) % RAW, 0, n // RAW + 1
    if n < 4 + GU:
        s = (n - 4) % RAW
        return s, LOADS_GROUP[s], LOADS_FIRST[s] + (n - 4) // RAW + 1
    c = n - BRANCH_ROW
    s = (c + 2) % RAW
    return s, 0, LOADS_FIRST[s] + NG * LOADS_GROUP[s] + c // RAW


def sq_slot(e):
    return 0 if e == 0 else 1 + (e - 1) % 5


def freed_by(u):
    return 4 if u < 3 else T[UNIT_TILES[u - 3]] + 1


def unit_of(j):
    return j // 2 if j < 8 else j - 4


def build(nc, x_d, w_d, par_d, up_d, fin_d, cos_d, sin_d, lmask_d, cmask_d, gmask_d, ident_d, out_d, gate_d, xkeep_d):
    with ExitStack() as ctx:
        def sb(name, shape, dt=F32):
            return ctx.enter_context(nc.sbuf_tensor(name, shape, dt))

        def bank(name):
            return ctx.enter_context(nc.psum_tensor(name, [P, S], F32))

        def sig(name, per, credit=0):
            return Signal(ctx.enter_context(nc.semaphore(name)), per, credit)

        big = sb("big", [P, KT, S])
        x, wt = big, big[:, 4:8, :]
        raw, rot = big[:, 0:2, :], big[:, 2:4, :]
        wt1 = big[:, 0:4, :]
        hh = sb("hh", [P, KT, S], F32R)
        hl = sb("hl", [P, KT, S], F32R)
        y = sb("y", [P, 3 * NG, S])
        raw_w = sb("raw_w", [P, RAW, 8, P])
        wh = sb("wh", [P, SPLIT, 8, P], F32R)
        wl = sb("wl", [P, SPLIT, 8, P], F32R)
        par = sb("par", [P, NPAR])
        up = sb("up", [P, P + 1])
        sc = sb("sc", [P, 8])
        with nc.sbuf_tensor("group", [P, 3 * NG, S], F32) as group:
            pass
        yl = sb("yl", [P, 3 * NG, S], F32R)
        v = group[:, 0:3, :].rearrange("p a s -> p (a s)").rearrange("p (b c) -> p b c", b=QB)
        sg = group[:, 3:6, :]
        cum = group[:, 6, :]
        rest = group[:, 7, :]
        qhat = group[:, 8, :]
        kend = group[:, 9, :].rearrange("p (b c) -> p b c", b=QB)
        rr = group[:, 10:12, :]
        rx, attsum = rr[:, 0, :], rr[:, 1, :]
        junk = rr[:, 1, 0:HD]
        sqa, sqb = rest, cum
        low = sb("low", [2 * RANK, S])
        total = sb("total", [P, NC])
        decay = sb("decay", [P, NC])
        att = sb("att", [P, 2, S])
        state = sb("state", [P, NC, DV])
        yh = sb("yh", [P, 3 * NG, S], F32R)
        qs, ks, kl = yh[:, 0:4, :], yh[:, 4:8, :], yh[:, 8:10, :]
        six = sb("six", [P, 6, S])
        probs, sneg = six[:, 0:4, :], six[:, 4:6, :]
        gates = six[:, :, :].rearrange("p (n g) s -> p n g s", n=2)
        w = sb("w", [P, 2, S])
        za = w
        negmax = sb("negmax", [P, 16])
        sums = sb("sums", [P, 16])
        rs = sb("rs", [P, 16])
        gstage = sb("gstage", [P, 2, S])
        cos = sb("cos", [P, S])
        sin = sb("sin", [P, S])
        lmask = sb("lmask", [P, 2 * S - P])
        cmask = sb("cmask", [P, S])
        gmask = sb("gmask", [P, 2, P], U32)
        ident = sb("ident", [P, P])
        mean = sb("mean", [P, P])
        cst = sb("cst", [P, 2])
        fin = sb("fin", [P, KT])

        proj = [bank("proj0"), bank("proj1")]
        score = [bank("score0"), bank("score1")]
        turn = [bank("turn0"), bank("turn1")]
        obank, mbank = bank("obank"), bank("mbank")
        zbanks = score + turn + [obank, mbank]

        s_x = [sig(f"s_x{n}", 16) for n in range(4)]
        s_const = sig("s_const", 16 * 7)
        s_par = sig("s_par", 16)
        s_up = sig("s_up", 16)
        loaded = [sig(f"loaded{s}", 16 * LOADS_LAYER[s]) for s in range(RAW)]
        s_init = sig("s_init", 0)
        s_passed = sig("s_passed", 0)
        tile_done = sig("tile_done", LAYER_TILES, LAYER_TILES)
        xsum_done = sig("xsum_done", 2)
        gate_done = sig("gate_done", 1)
        glaatt_done = sig("glaatt_done", 1)
        kturn_done = sig("kturn_done", 1)
        upd_done = sig("upd_done", 1)
        score_done = sig("score_done", 16)
        turn_done = sig("turn_done", 12)
        out_done = sig("out_done", 5)
        act_free = sig("act_free", len(BY_ACT) * NG, 2)
        xsq_done = sig("xsq_done", KT)
        xr_done = sig("xr_done", 1)
        act_pre = sig("act_pre", 1)
        hh_ready = sig("hh_ready", KT)
        yh_c = sig("yh_c", NG)
        low_ready = sig("low_ready", 1)
        soft_ready = sig("soft_ready", 1, 1)
        lam_exp = sig("lam_exp", 1)
        decay_done = sig("decay_done", 4)
        qk_high = sig("qk_high", 2)
        tanh_done = sig("tanh_done", 3)
        kend_ready = sig("kend_ready", 1)
        exp_done = sig("exp_done", 16)
        wt_ready = sig("wt_ready", 12, 1)
        sq_done = sig("sq_done", 2)
        r_done = sig("r_done", 1)
        act_grp = sig("act_grp", 4)
        dve_free = sig("dve_free", len(BY_DVE) * NG)
        dve_pre = sig("dve_pre", 6)
        min_done = sig("min_done", 1)
        xacc_done = sig("xacc_done", KT - 2)
        t_ready = sig("t_ready", KT)
        h_even = sig("h_even", KT // 2)
        cum_ready = sig("cum_ready", 1)
        a_read = sig("a_read", 1)
        b_rotated = sig("b_rotated", 1)
        b_parts = sig("b_parts", 1)
        att_ready = sig("att_ready", 1)
        state_ready = sig("state_ready", 1)
        max_ready = sig("max_ready", 16)
        w_ready = sig("w_ready", 12)
        y_read = sig("y_read", 3, 1)
        dve_grp = sig("dve_grp", 35)
        ab_normed = sig("ab_normed", 1)
        yl_ready = sig("yl_ready", 3 * NG)
        z_read = sig("z_read", 24, 6)
        mixed = sig("mixed", 8, 2)
        dve_mix = sig("dve_mix", 24)
        x_ready = sig("x_ready", 8, 8)
        out_ready = sig("out_ready", 8)
        split_done = sig("split_done", ROWS_LAYER, RAW)
        yh_ab = sig("yh_ab", 2 * NG)
        c_rotated = sig("c_rotated", 1)
        c_parts = sig("c_parts", 1)
        pool_grp = sig("pool_grp", 5)
        h_odd = sig("h_odd", KT // 2)
        pool_high = sig("pool_high", ROWS_LAYER)
        swapped = sig("swapped", 2 * 64)
        gstored = [sig(f"gstored{s}", 3 * 16, 16) for s in range(2)]
        x_kept = sig("x_kept", 16)
        x_back = sig("x_back", 16)
        gloaded = [sig(f"gloaded{s}", 4 * 16) for s in range(2)]
        s_out = sig("s_out", 16)

        block = ctx.enter_context(nc.Block())

        def free_of(name, L, i):
            if name in BY_DVE:
                return dve_free.at(L, len(BY_DVE) * i + (BY_DVE.index(name) + 1))
            return act_free.at(L, len(BY_ACT) * i + (BY_ACT.index(name) + 1))

        def high_of_y(L, k):
            return yh_ab.at(L, k + 1) if k < 2 * NG else yh_c.at(L, k - 2 * NG + 1)

        def apart(eng):
            eng.sem_inc(s_passed.sem, 1)

        @block.sync
        def _(sp):
            for n in range(4):
                t = slice(2 * n, 2 * n + 2)
                sp.dma_start(x[:, t, :], x_d[:, t, :]).then_inc(s_x[n].sem, 16)

            def unit(L, row, slot):
                sp.dma_start(raw_w[:, slot, :, :], w_d[L * ROWS_LAYER + row, :, :].rearrange(
                    "p (t c) -> p t c", c=P)).then_inc(loaded[slot].sem, 16)

            with sp.Fori(0, DEPTH) as L:
                sp.wait_ge(*y_read.at(L * NG, 0))
                sp.dma_start(par[:, :], par_d[L, :, :]).then_inc(s_par.sem, 16)
                for n in range(RAW + 1):
                    sp.wait_ge(*split_done.at(L, n + 1 - RAW))
                    unit(L, n, arrival(n)[0])
                sp.wait_ge(*x_ready.at(L, 0))
                for n in range(4):
                    sp.wait_ge(*s_x[n].at(0, 16))
                sp.dma_start(xkeep_d, x[:, :, :]).then_inc(x_kept.sem, 16)
                with sp.Fori(0, NG) as i:
                    sp.wait_ge(*soft_ready.at(L * NG + i, 0))
                    sp.dma_start(up[:, :], up_d[L * NG + i, :, :]).then_inc(s_up.sem, 16)
                    for j in range(GU):
                        last = 4 + j - RAW if j >= RAW else 4 + max(n for n in range(GU) if n % RAW == j) - GU
                        sp.wait_ge(*split_done.at(L, i * GU + (last + 1)))
                        unit(L, i * GU + (4 + j), arrival(4 + j)[0])
                for row in range(BRANCH_ROW + RAW, ROWS_LAYER):
                    sp.wait_ge(*split_done.at(L, row - RAW + 1))
                    unit(L, row, arrival(row)[0])
                    if row == BRANCH_ROW + 8:
                        sp.wait_ge(*tile_done.at(L, BRANCH_TILE + 1))
                        sp.wait_ge(*x_kept.at(L + 1, 0))
                        sp.dma_start(x[:, :, :], xkeep_d).then_inc(x_back.sem, 16)
            for k in range(KT):
                sp.wait_ge(*out_ready.at(0, k + 1))
                sp.dma_start(out_d[:, k, :], y[:, k, :]).then_inc(s_out.sem, 16)
            sp.wait_ge(*s_out.at(0, 16 * KT))

        @block.gpsimd
        def _(pool):
            pool.sem_inc(split_done.sem, RAW)

            def split(L, i, n, slot, free):
                s, per_group, count = arrival(n)
                src = raw_w[:, s, :, :]
                pool.wait_ge(*loaded[s].at(L, 16 * (i * per_group + count)))
                pool.wait_ge(*tile_done.at(L, free))
                apart(pool)
                pool.tensor_scalar(wh[:, slot, :, :], src, 1.0, 1.0, ALU.mult, ALU.mult).then_inc(pool_high.sem, 1)
                pool.wait_ge(*pool_high.at(L, i * GU + (n + 1)))
                apart(pool)
                pool.tensor_tensor(wl[:, slot, :, :], src, wh[:, slot, :, :].bitcast(F32), ALU.subtract).then_inc(split_done.sem, 1)

            with pool.Fori(0, DEPTH) as L:
                for n in range(4):
                    split(L, 0, n, OUT_SLOT[n], OUT_TILE + 5 + n - LAYER_TILES)

                for k in range(1, KT, 2):
                    pool.wait_ge(*hh_ready.at(L, k + 1))
                    apart(pool)
                    pool.tensor_tensor(hl[:, k, :], six[:, k % 6, :], hh[:, k, :].bitcast(F32), ALU.subtract).then_inc(h_odd.sem, 1)

                def tiles(i):
                    G = L * NG + i
                    grp = Chain(pool, pool_grp, G)
                    for u in range(3, GU):
                        if u == 3 + UNIT_TILES.index("m0"):
                            pool.wait_ge(*swapped.at(G, 2 * 64))
                            apart(pool)
                            grp.did(pool.tensor_tensor(raw[:, :, :], raw[:, :, :], cos[:, :].unsqueeze(1).to_broadcast([P, 2, S]), ALU.mult))
                            grp.did(pool.tensor_tensor(rot[:, :, :], rot[:, :, :], sin[:, :].unsqueeze(1).to_broadcast([P, 2, S]), ALU.mult))
                            grp.last()
                            apart(pool)
                            pool.tensor_tensor(raw[:, :, :], raw[:, :, :], rot[:, :, :], ALU.add).then_inc(c_rotated.sem, 1)
                        if u == 3 + UNIT_TILES.index("m2"):
                            pool.wait_ge(*qk_high.at(G, 2))
                            pool.wait_ge(*split_done.at(L, i * GU + (u + 1)))
                            up_rows, low_rows = slice(0, HD), slice(HD, P)
                            for own, other, m in ((up_rows, low_rows, 2), (low_rows, up_rows, 3)):
                                apart(pool)
                                grp.did(pool.tensor_tensor(qs[other, m, :], raw[own, 0, :], qs[own, m, :].bitcast(F32), ALU.subtract))
                                grp.last()
                            apart(pool)
                            grp.did(pool.tensor_tensor(kl[up_rows, 1, :], raw[up_rows, 1, :], ks[up_rows, 2, :].bitcast(F32), ALU.subtract))
                            grp.last()
                            apart(pool)
                            pool.tensor_tensor(kl[low_rows, 1, :], raw[low_rows, 1, :], ks[low_rows, 3, :].bitcast(F32), ALU.subtract).then_inc(c_parts.sem, 1)
                            pool.wait_ge(*c_parts.at(G, 1))
                        before = [t for t in range(u) if SLOT[t] == SLOT[u]]
                        split(L, i, 1 + u, SLOT[u], i * NT + (1 + (freed_by(before[-1]) if before else 0)))

                with pool.Fori(0, NG - 1) as i:
                    tiles(i)
                    for u in range(3):
                        last = max(t for t in range(GU) if SLOT[t] == SLOT[u])
                        split(L, i, 1 + GU + u, SLOT[u], i * NT + (1 + freed_by(last)))
                tiles(NG - 1)
                for c in range(12):
                    if c == BRANCH_SLOTS:
                        pool.wait_ge(*ab_normed.at((L + 1) * NG, 0))
                        apart(pool)
                        for k in range(2 * NG):
                            pool.tensor_scalar(yh[:, k, :], y[:, k, :], 1.0, 1.0, ALU.mult, ALU.mult).then_inc(yh_ab.sem, 1)
                    last = (NG - 1) * NT + 1 + freed_by(GU - 4 + c) if c < BRANCH_SLOTS else BRANCH_TILE + 2 * (c - BRANCH_SLOTS + 1)
                    split(L, 0, BRANCH_ROW + c, SLOT[c % BRANCH_SLOTS], last)
                for o in range(8):
                    last = BRANCH_TILE if o == 0 else BRANCH_TILE + 2 * (9 + o) if o < SPLIT else OUT_TILE + o - SPLIT + 1
                    split(L, 0, OUT_ROW + o, OUT_SLOT[o % SPLIT], last)

        @block.scalar
        def _(act):
            act.sem_inc(act_free.sem, 2)
            act.sem_inc(wt_ready.sem, 1)
            act.sem_inc(soft_ready.sem, 1)
            for s in range(2):
                act.sem_inc(gstored[s].sem, 16)
            act.wait_ge(*s_init.at(0, 1))

            def square_of_x(n, e):
                act.wait_ge(*x_ready.at(n - 1, e + 1))
                if e >= 6:
                    act.wait_ge(*xacc_done.at(n, e - 5))
                act.activation(six[:, sq_slot(e), :], x[:, e, :], ACT.Square).then_inc(xsq_done.sem, 1)

            def rsqrt_of_x(n):
                act.wait_ge(*xsum_done.at(n, 2))
                act.activation(rx, mbank[:, :], ACT.Ln, bias=cst[:, 0:1], scale=P / D).then_inc(act_pre.sem, 1)
                act.wait_ge(*act_pre.at(n, 1))
                act.activation(rx, rx, ACT.Exp, scale=-0.5).then_inc(xr_done.sem, 1)

            for e in range(KT):
                act.wait_ge(*s_x[e // 2].at(0, 16))
                square_of_x(0, e)
            for dst, src in ((cmask[:, :], cmask_d), (cos[:, :], cos_d), (sin[:, :], sin_d), (gmask[:, :, :], gmask_d),
                             (ident[:, :], ident_d), (lmask[:, :], lmask_d), (fin[:, :], fin_d)):
                act.dma_start(dst, src).then_inc(s_const.sem, 16)
            with act.Fori(0, DEPTH) as L:
                rsqrt_of_x(L)
                act.wait_ge(*dve_pre.at(L, 2))
                act.activation(sc[:, 0:2], sc[:, 0:2], ACT.Exp).then_inc(lam_exp.sem, 1)
                for k in range(KT):
                    act.wait_ge(*t_ready.at(L, k + 1))
                    act.activation(hh[:, k, :], six[:, k % 6, :], ACT.Copy).then_inc(hh_ready.sem, 1)
                act.wait_ge(*tile_done.at(L, 1))
                act.activation(low[:, :], proj[1][0:2 * RANK, :], ACT.Copy).then_inc(low_ready.sem, 1)

                def load_gates(d):
                    for s in range(2):
                        act.wait_ge(*gstored[s].at((L + 1) * NG, 0))
                    act.dma_start(gates[:, d % 2, :, :], gate_d[3 * d:3 * d + 3, :, :].rearrange(
                        "g p s -> p g s")).then_inc(gloaded[d % 2].sem, 16)

                with act.Fori(0, NG) as i:
                    G = L * NG + i
                    grp = Chain(act, act_grp, G)

                    def have(name):
                        act.wait_ge(*tile_done.at(L, i * NT + (T[name] + 2)))

                    def free(ins):
                        return ins.then_inc(act_free.sem, 1)

                    def values_out(b):
                        have(f"v{b}")
                        free(act.activation(v[:, b, :], proj[b % 2][:, 0:3 * P], ACT.Copy))

                    values_out(0)
                    act.wait_ge(*min_done.at(G, 1))
                    grp.did(act.activation(qhat, turn[0][:, :], ACT.Abs, bias=up[:, P:P + 1]))
                    grp.last()
                    grp.did(act.activation(qhat, qhat, ACT.Exp, scale=-1.0))
                    grp.last()
                    act.activation(qhat, qhat, ACT.Ln, bias=cst[:, 1:2]).then_inc(soft_ready.sem, 1)
                    values_out(1)
                    act.wait_ge(*cum_ready.at(G, 1))
                    act.activation(qhat, cum, ACT.Exp, scale=1 / TAU).then_inc(decay_done.sem, 1)
                    act.activation(rest, rest, ACT.Exp, scale=1 / TAU).then_inc(decay_done.sem, 1)
                    act.activation(decay[:, :], total[:, :], ACT.Exp, scale=1 / TAU).then_inc(decay_done.sem, 1)
                    act.wait_ge(*decay_done.at(G, 1))
                    act.activation(cum, cum, ACT.Exp, scale=-1 / TAU).then_inc(decay_done.sem, 1)
                    for b in range(2, QB):
                        values_out(b)
                    act.wait_ge(*x_kept.at(L, 16))
                    have("a")
                    up_rows, low_rows = slice(0, DK), slice(DK, P)
                    for m, src in enumerate((up_rows, low_rows)):
                        for dst in (up_rows, low_rows):
                            ins = act.activation(raw[dst, m, :], proj[T["a"] % 2][src, :], ACT.Copy, scale=(DK ** -0.5, 1.0)[m])
                    free(ins)

                    def high_parts(n):
                        act.wait_ge(*(b_rotated, c_rotated)[n].at(G, 1))
                        t = (w, raw)[n]
                        up_rows, low_rows = slice(0, HD), slice(HD, P)
                        for own, other, m in ((up_rows, low_rows, 2 * n), (low_rows, up_rows, 2 * n + 1)):
                            act.activation(qs[own, m, :], t[own, 0, :], ACT.Copy)
                            act.activation(ks[own, m, :], t[own, 1, :], ACT.Copy)
                            ins = act.activation(ks[other, m, :], t[own, 1, :], ACT.Copy)
                        ins.then_inc(qk_high.sem, 1)

                    def unrotated(m, name):
                        have(name)
                        free(act.activation(raw[:, m, :], proj[T[name] % 2][:, :], ACT.Copy, scale=(HD ** -0.5, 1.0)[m]))

                    def swap_halves(key):
                        act.wait_ge(*free_of(key, L, i))
                        for a in range(4):
                            b = a ^ 1
                            act.dma_start(rot[32 * a:32 * a + 32, :, :], raw[32 * b:32 * b + 32, :, :]).then_inc(swapped.sem, 16)

                    act.wait_ge(*a_read.at(G, 1))
                    unrotated(0, "bq")
                    unrotated(1, "bk")
                    swap_halves("bk")
                    act.wait_ge(*b_rotated.at(G, 1))
                    unrotated(0, "cq")
                    high_parts(0)
                    unrotated(1, "ck")
                    act.wait_ge(*kturn_done.at(G, 1))
                    act.activation(kend[:, :, :], turn[0][:, :].rearrange("p (b c) -> p b c", b=QB), ACT.Copy).then_inc(kend_ready.sem, 1)
                    swap_halves("ck")

                    def tanh_gate(k, name):
                        have(name)
                        act.activation(sg[:, k, :], proj[T[name] % 2][:, :], ACT.Tanh, scale=0.5).then_inc(tanh_done.sem, 1)

                    def merge_gate(m):
                        have(f"m{m}")
                        act.wait_ge(*gstored[m % 2].at(G, 16 * (m // 2)))
                        free(act.activation(gstage[:, m % 2, :], proj[T[f"m{m}"] % 2][:, :], ACT.Tanh, scale=0.5))
                        act.wait_ge(*free_of(f"m{m}", L, i))
                        act.dma_start(gate_d[i * 6 + m, :, :], gstage[:, m % 2, :]).then_inc(gstored[m % 2].sem, 16)

                    def exp(j):
                        act.wait_ge(*max_ready.at(G, j + 1))
                        if j >= 4:
                            act.wait_ge(*w_ready.at(G, unit_of(j - 4) + 1))
                        src, k = (score[j % 2][:, :], 1.0) if j < 8 else (sneg[:, j % 2, :], -1.0)
                        act.activation(probs[:, j % 4, :], src, ACT.Exp, bias=negmax[:, j:j + 1], scale=k,
                                       accum_out=sums[:, j:j + 1]).then_inc(exp_done.sem, 1)

                    def turned(u):
                        act.wait_ge(*turn_done.at(G, u + 1))
                        if u == 4:
                            act.wait_ge(*out_done.at(G, 3))
                        q = (u if u < 4 else (u - 4) // 2) * P
                        act.activation((wt if u < 4 or u % 2 == 0 else wt1)[:, :, q:q + P], turn[u % 2][:, :].rearrange("p (k q) -> p k q", k=QB),
                                       ACT.Copy).then_inc(wt_ready.sem, 1)

                    tanh_gate(0, "ag")
                    tanh_gate(1, "bg")
                    exp(0)
                    exp(1)
                    high_parts(1)
                    act.wait_ge(*out_done.at(G, 1))
                    act.activation(sqa[:, :], obank[:, :], ACT.Square).then_inc(sq_done.sem, 1)
                    for u in range(4):
                        exp(2 * u + 2)
                        exp(2 * u + 3)
                        turned(u)
                        if u == 0:
                            tanh_gate(2, "cg")
                        if u >= 2:
                            merge_gate(u - 2)
                    act.wait_ge(*out_done.at(G, 3))
                    act.activation(sqb[:, :], obank[:, :], ACT.Square).then_inc(sq_done.sem, 1)
                    for u in range(4, 10):
                        exp(u + 6)
                        turned(u)
                        if u == 5:
                            merge_gate(2)
                            act.wait_ge(*out_done.at(G, 2))
                            grp.did(act.activation(rr[:, 0, :], mbank[:, :], ACT.Ln, bias=cst[:, 0:1]))
                            act.wait_ge(*out_done.at(G, 4))
                            grp.did(act.activation(rr[:, 1, :], obank[:, :], ACT.Ln, bias=cst[:, 0:1]))
                            grp.last()
                            act.activation(rr[:, :, :], rr[:, :, :], ACT.Exp, scale=-0.5).then_inc(r_done.sem, 1)
                        if u == 7:
                            merge_gate(3)
                        if u == 9:
                            merge_gate(4)
                    turned(10)
                    turned(11)
                    merge_gate(5)
                    grp.close()

                act.wait_ge(*y_read.at((L + 1) * NG, 0))
                load_gates(0)
                load_gates(1)
                for k in range(2 * NG, 3 * NG):
                    act.activation(yh[:, k, :], y[:, k, :], ACT.Copy).then_inc(yh_c.sem, 1)
                for d in range(2, KT):
                    act.wait_ge(*mixed.at(L, d - 1))
                    load_gates(d)
                for s in range(2):
                    act.wait_ge(*gloaded[s].at(L + 1, 0))
                for e in range(KT):
                    square_of_x(L + 1, e)

            rsqrt_of_x(DEPTH)

        @block.vector
        def _(dve):
            dve.sem_inc(y_read.sem, 1)
            dve.sem_inc(z_read.sem, 6)
            dve.sem_inc(x_ready.sem, 8)
            dve.sem_inc(mixed.sem, 2)
            for t, val in ((mean[:, :], 1 / P), (cst[:, 0:1], EPS), (cst[:, 1:2], 1.0),
                           (state[:, :, :], 0.0), (att[:, :, :], 0.0)):
                last = dve.memset(t, val)
            last.then_inc(s_init.sem, 1)
            dve.wait_ge(*s_init.at(0, 1))

            def add_square(n, e):
                dve.wait_ge(*xsq_done.at(n, e + 1))
                if e >= 2:
                    dve.wait_ge(*xacc_done.at(n, e - 1))
                dve.tensor_tensor(six[:, 0, :], six[:, 0, :], six[:, sq_slot(e), :], ALU.add).then_inc(xacc_done.sem, 1)

            for e in range(1, KT - 1):
                add_square(0, e)

            def normed(L, k, dst, g):
                return dve.scalar_tensor_tensor(dst, x[:, k, :], g[:, k:k + 1], rx, ALU.mult, ALU.mult)

            with dve.Fori(0, DEPTH) as L:
                chain = Chain(dve, dve_pre, L)
                dve.wait_ge(*s_par.at(L, 16))
                dl = par[:, C_DL:C_DL + 4 * HD].rearrange("p (n d) -> p n d", n=4)
                apart(dve)
                chain.did(dve.tensor_tensor_reduce(junk[:, :], dl[:, 0, :], dl[:, 1, :], 1.0, 0.0, ALU.mult, ALU.add, sc[:, 0:1]))
                chain.last()
                apart(dve)
                chain.did(dve.tensor_tensor_reduce(junk[:, :], dl[:, 2, :], dl[:, 3, :], 1.0, 0.0, ALU.mult, ALU.add, sc[:, 1:2]))
                dve.wait_ge(*xr_done.at(L, 1))

                def low_part(k):
                    dve.wait_ge(*hh_ready.at(L, k + 1))
                    dve.tensor_tensor(hl[:, k, :], six[:, k % 6, :], hh[:, k, :].bitcast(F32), ALU.subtract).then_inc(h_even.sem, 1)

                for k in range(KT):
                    if k >= 6:
                        dve.wait_ge(*(h_odd if k % 2 else h_even).at(L, 1))
                    normed(L, k, six[:, k % 6, :], par[:, C_NG:C_NG + KT]).then_inc(t_ready.sem, 1)
                    if k % 2:
                        low_part(k - 1)
                dve.wait_ge(*s_const.at(1, 0))
                dve.wait_ge(*lam_exp.at(L, 1))
                chain.did(dve.tensor_tensor(sc[:, 2:3], sc[:, 1:2], sc[:, 0:1], ALU.subtract))
                chain.last()
                chain.did(dve.tensor_tensor(sc[:, 2:3], sc[:, 2:3], par[:, C_LI:C_LI + 1], ALU.subtract))
                chain.did(dve.tensor_scalar(sc[:, 3:4], par[:, C_GA:C_GA + 1], 0.5, None, ALU.mult))
                chain.did(dve.tensor_scalar(sc[:, 4:5], par[:, C_GD:C_GD + 1], par[:, C_LI + 1:C_LI + 2], 0.5, ALU.mult, ALU.mult))
                chain.last()
                chain.close()
                apart(dve)

                with dve.Fori(0, NG) as i:
                    G = L * NG + i
                    grp = Chain(dve, dve_grp, G)
                    dve.wait_ge(*wt_ready.at(G, 0))

                    def have(name):
                        dve.wait_ge(*tile_done.at(L, i * NT + (T[name] + 2)))

                    def free(ins):
                        return ins.then_inc(dve_free.sem, 1)

                    dve.wait_ge(*gate_done.at(G, 1))
                    dve.tensor_scalar(rest, turn[0][:, :], up[:, P:P + 1], 0.0, ALU.add, ALU.min).then_inc(min_done.sem, 1)
                    dve.wait_ge(*soft_ready.at(G, 1))
                    grp.did(dve.tensor_tensor(rest, rest, qhat, ALU.subtract))
                    grp.last()
                    f, b = slice(0, DK), slice(DK, P)
                    grp.did(dve.tensor_tensor_scan(cum[f, :], cmask[f, :], rest[f, :], 0.0, ALU.mult, ALU.add))
                    grp.did(dve.tensor_tensor_scan(cum[b, ::-1], cmask[b, ::-1], rest[b, ::-1], 0.0, ALU.mult, ALU.add))
                    grp.last()
                    cumc = cum.rearrange("p (n c) -> p n c", n=NC)
                    grp.did(dve.tensor_copy(total[f, :], cumc[f, :, CH - 1]))
                    grp.did(dve.tensor_copy(total[b, :], cumc[b, :, 0]))
                    grp.last()
                    dve.tensor_tensor(rest.rearrange("p (n c) -> p n c", n=NC),
                                      total[:, :].unsqueeze(2).to_broadcast([P, NC, CH]), cumc, ALU.subtract).then_inc(cum_ready.sem, 1)
                    dve.wait_ge(*free_of("a", L, i))
                    dve.wait_ge(*decay_done.at(G, 4))
                    for t, m in ((qhat, 0), (cum, 1), (rest, 1)):
                        ins = dve.tensor_tensor(t, raw[:, m, :], t, ALU.mult)
                    ins.then_inc(a_read.sem, 1)

                    dve.wait_ge(*swapped.at(G, 64))
                    grp.did(dve.tensor_tensor(raw[:, :, :], raw[:, :, :], cos[:, :].unsqueeze(1).to_broadcast([P, 2, S]), ALU.mult))
                    grp.did(dve.tensor_tensor(rot[:, :, :], rot[:, :, :], sin[:, :].unsqueeze(1).to_broadcast([P, 2, S]), ALU.mult))
                    grp.last()
                    dve.tensor_tensor(w[:, :, :], raw[:, :, :], rot[:, :, :], ALU.add).then_inc(b_rotated.sem, 1)
                    dve.wait_ge(*qk_high.at(G, 1))
                    up_rows, low_rows = slice(0, HD), slice(HD, P)
                    for own, other, m in ((up_rows, low_rows, 0), (low_rows, up_rows, 1)):
                        dve.tensor_tensor(qs[other, m, :], w[own, 0, :], qs[own, m, :].bitcast(F32), ALU.subtract)
                        ins = dve.tensor_tensor(kl[own, 0, :], w[own, 1, :], ks[own, m, :].bitcast(F32), ALU.subtract)
                    ins.then_inc(b_parts.sem, 1)

                    def silu(k, name):
                        dve.wait_ge(*tanh_done.at(G, k + 1))
                        free(dve.scalar_tensor_tensor(sg[:, k, :], sg[:, k, :], 1.0, proj[T[name] % 2][:, :], ALU.add, ALU.mult))

                    silu(0, "ag")
                    dve.wait_ge(*glaatt_done.at(G, 1))
                    apart(dve)
                    for n in range(2):
                        ins = dve.copy_predicated(att[:, n, :].rearrange("p (b c) -> p b c", b=QB),
                                                  gmask[:, n, :].unsqueeze(1).to_broadcast([P, QB, P]),
                                                  score[n][:, :].rearrange("p (b c) -> p b c", b=QB))
                    grp.did(ins)
                    grp.last()
                    dve.tensor_tensor(attsum[:, :], att[:, 0, :], att[:, 1, :], ALU.add).then_inc(att_ready.sem, 1)
                    dve.wait_ge(*upd_done.at(G, 1))

                    def update(n):
                        return (mbank if n % 2 else turn[1])[:, (n // 2) * DV:(n // 2 + 1) * DV]

                    for n in range(NC - 1):
                        r = NC - 1 - n
                        if n:
                            grp.last()
                        dve.scalar_tensor_tensor(state[f, n + 1, :], state[f, n, :], decay[f, n:n + 1], update(n)[f, :], ALU.mult, ALU.add)
                        ins = dve.scalar_tensor_tensor(state[b, r - 1, :], state[b, r, :], decay[b, r:r + 1], update(r)[b, :], ALU.mult, ALU.add)
                        if n < NC - 2:
                            grp.did(ins)
                    ins.then_inc(state_ready.sem, 1)
                    silu(1, "bg")

                    def row_max(j):
                        dve.wait_ge(*score_done.at(G, j + 1))
                        if j < 8:
                            dve.tensor_reduce(negmax[:, j:j + 1], score[j % 2][:, :], AX_X, ALU.max, negate=True).then_inc(max_ready.sem, 1)
                        else:
                            b = (j - 8) // 2
                            if j >= 10:
                                dve.wait_ge(*exp_done.at(G, j - 1))
                            apart(dve)
                            dve.tensor_tensor_reduce(sneg[:, j % 2, :], score[j % 2][:, :], lmask[:, S - P - P * b:2 * S - P - P * b], -1.0, 3.0e38,
                                                     ALU.add, ALU.min, negmax[:, j:j + 1]).then_inc(max_ready.sem, 1)

                    def weights(u):
                        if u >= 2:
                            dve.wait_ge(*turn_done.at(G, u - 1))
                        if u < 4:
                            a, c = 2 * u, 2 * u + 1
                            dve.wait_ge(*exp_done.at(G, c + 1))
                            grp.did(dve.reciprocal(rs[:, a:a + 2], sums[:, a:a + 2]))
                            grp.last()
                            grp.did(dve.tensor_tensor(rs[:, c:c + 1], rs[:, c:c + 1], sc[:, 2:3], ALU.mult))
                            grp.did(dve.tensor_scalar(w[:, u % 2, :], probs[:, a % 4, :], rs[:, a:a + 1], None, ALU.mult))
                            grp.last()
                            dve.scalar_tensor_tensor(w[:, u % 2, :], probs[:, c % 4, :], rs[:, c:c + 1], w[:, u % 2, :],
                                                     ALU.mult, ALU.add).then_inc(w_ready.sem, 1)
                        else:
                            j = u + 4
                            dve.wait_ge(*exp_done.at(G, j + 1))
                            grp.did(dve.reciprocal(rs[:, j:j + 1], sums[:, j:j + 1]))
                            grp.last()
                            dve.tensor_scalar(w[:, u % 2, :], probs[:, j % 4, :], rs[:, j:j + 1], None, ALU.mult).then_inc(w_ready.sem, 1)

                    row_max(0)
                    row_max(1)
                    dve.wait_ge(*b_parts.at(G, 1))
                    dve.wait_ge(*sq_done.at(G, 1))
                    dve.scalar_tensor_tensor(y[:, i, :], obank[:, :], sc[:, 3:4], sg[:, 0, :], ALU.mult, ALU.mult).then_inc(y_read.sem, 1)
                    for u in range(4):
                        row_max(2 * u + 2)
                        row_max(2 * u + 3)
                        weights(u)
                        if u == 1:
                            silu(2, "cg")
                    row_max(10)
                    weights(4)
                    dve.wait_ge(*sq_done.at(G, 2))
                    dve.scalar_tensor_tensor(y[:, NG + i, :], obank[:, :], sc[:, 4:5], sg[:, 1, :], ALU.mult, ALU.mult).then_inc(y_read.sem, 1)
                    for u in range(5, 12):
                        if u < 10:
                            row_max(u + 6)
                        weights(u)
                        if u == 8:
                            dve.wait_ge(*r_done.at(G, 1))
                            dve.wait_ge(*y_read.at(G, 2))
                            grp.did(dve.tensor_tensor(y[:, i, :], y[:, i, :], rr[:, 0, :], ALU.mult))
                            dve.tensor_tensor(y[:, NG + i, :], y[:, NG + i, :], rr[:, 1, :], ALU.mult).then_inc(ab_normed.sem, 1)
                    dve.wait_ge(*out_done.at(G, 5))
                    dve.scalar_tensor_tensor(y[:, 2 * NG + i, :], mbank[:, :], 0.5, sg[:, 2, :], ALU.mult, ALU.mult).then_inc(y_read.sem, 1)
                    dve.wait_ge(*y_read.at(G, 3))
                    grp.close()

                for k in range(3 * NG):
                    dve.wait_ge(*high_of_y(L, k))
                    dve.tensor_tensor(yl[:, k, :], y[:, k, :], yh[:, k, :].bitcast(F32), ALU.subtract).then_inc(yl_ready.sem, 1)

                mix = Chain(dve, dve_mix, L)
                for d in range(KT):
                    dve.wait_ge(*gloaded[d % 2].at(L, 16 * (d // 2 + 1)))
                    for g in range(3):
                        zt = 3 * d + g
                        dve.wait_ge(*tile_done.at(L, BRANCH_TILE + zt + 1))
                        if g == 0 and d:
                            dve.wait_ge(*mixed.at(L, d))
                        dst = za[:, 0, :] if g == 0 else za[:, 1, :]
                        if g == 2:
                            mix.last()
                        dve.scalar_tensor_tensor(dst, gates[:, d % 2, g, :], 1.0, zbanks[zt % 6][:, :], ALU.add, ALU.mult).then_inc(z_read.sem, 1)
                        if g == 1:
                            dve.wait_ge(*z_read.at(L, zt + 1))
                            mix.did(dve.tensor_tensor(za[:, 0, :], za[:, 0, :], za[:, 1, :], ALU.add))
                    dve.wait_ge(*z_read.at(L, 3 * d + 3))
                    mix.did(dve.tensor_tensor(hh[:, d, :], za[:, 0, :], za[:, 1, :], ALU.add))
                    mix.did(dve.tensor_tensor(za[:, 0, :], za[:, 0, :], za[:, 1, :], ALU.add))
                    mix.last()
                    dve.tensor_tensor(hl[:, d, :], za[:, 0, :], hh[:, d, :].bitcast(F32), ALU.subtract).then_inc(mixed.sem, 1)
                mix.close()
                dve.wait_ge(*x_back.at(L, 16))
                for e in range(KT):
                    dve.wait_ge(*tile_done.at(L, OUT_TILE + e + 1))
                    dve.scalar_tensor_tensor(x[:, e, :], proj[e % 2][:, :], 0.5, x[:, e, :], ALU.mult, ALU.add).then_inc(x_ready.sem, 1)
                    if e >= 2:
                        add_square(L + 1, e - 1)
                dve.wait_ge(*x_ready.at(L + 1, 0))
                apart(dve)

            dve.wait_ge(*xr_done.at(DEPTH, 1))
            for k in range(KT):
                normed(DEPTH, k, y[:, k, :], fin).then_inc(out_ready.sem, 1)

        @block.tensor
        def _(pe):
            pe.sem_inc(tile_done.sem, LAYER_TILES)
            pe.wait_ge(*s_init.at(0, 1))

            def x_mean(n):
                pe.wait_ge(*xacc_done.at(n, KT - 2))
                pe.matmul(mbank[:, :], mean[:, :], six[:, sq_slot(0), :], start=True, stop=False).then_inc(xsum_done.sem, 1)
                pe.wait_ge(*xsq_done.at(n, KT))
                pe.matmul(mbank[:, :], mean[:, :], six[:, sq_slot(KT - 1), :], start=False, stop=True).then_inc(xsum_done.sem, 1)

            def product(dst, slot, ks):
                for k in ks:
                    for a, b in ((wh, hh), (wh, hl), (wl, hh)):
                        last = pe.matmul(dst, a[:, slot, k, :], b[:, k, :], start=(k == 0 and a is wh and b is hh),
                                         stop=(k == KT - 1 and a is wl))
                return last

            x_mean(0)
            with pe.Fori(0, DEPTH) as L:
                pe.wait_ge(*split_done.at(L, 1))
                for k in range(KT + 1):
                    if k < KT:
                        pe.wait_ge(*hh_ready.at(L, k + 1))
                        for a in (wh, wl):
                            pe.matmul(proj[1][:, :], a[:, 3, k, :], hh[:, k, :], start=(k == 0 and a is wh), stop=False)
                    if k:
                        pe.wait_ge(*(h_odd if (k - 1) % 2 else h_even).at(L, (k - 1) // 2 + 1))
                        last = pe.matmul(proj[1][:, :], wh[:, 3, k - 1, :], hl[:, k - 1, :], start=False, stop=(k == KT))
                last.then_inc(tile_done.sem, 1)
                pe.wait_ge(*s_const.at(1, 0))
                apart(pe)

                with pe.Fori(0, NG) as i:
                    G = L * NG + i

                    def arrived(u):
                        pe.wait_ge(*split_done.at(L, i * GU + (u + 2)))

                    def bank_free(t):
                        if t >= 2:
                            pe.wait_ge(*free_of(TILES[t - 2], L, i))
                        else:
                            pe.wait_ge(*act_free.at(L, len(BY_ACT) * i + (t - 1)))

                    def project(name, ks=range(KT)):
                        t, u = T[name], 3 + UNIT_TILES.index(name)
                        if 0 in ks:
                            arrived(u)
                            bank_free(t)
                        last = product(proj[t % 2][:, :], SLOT[u], ks)
                        if KT - 1 in ks:
                            last.then_inc(tile_done.sem, 1)

                    filled = 0

                    def fill(steps):
                        nonlocal filled
                        while steps:
                            tile, k = divmod(filled, KT)
                            n = min(steps, KT - k)
                            project(FILLERS[tile], range(k, k + n))
                            filled, steps = filled + n, steps - n

                    arrived(2)
                    for b in range(QB):
                        bank_free(b)
                        for k in range(KT):
                            for n, (a, c) in enumerate(((hh, wh), (hh, wl), (hl, wh))):
                                last = pe.matmul(proj[b % 2][:, 0:3 * P], a[:, k, P * b:P * b + P], c[:, 0:3, k, :],
                                                 start=(k == 0 and n == 0), stop=(k == KT - 1 and n == 2))
                        last.then_inc(tile_done.sem, 1)
                        if b == 0:
                            pe.wait_ge(*s_up.at(G, 16))
                            pe.wait_ge(*low_ready.at(L, 1))
                            pe.matmul(turn[0][:, :], up[0:2 * RANK, 0:P], low[:, :], start=True, stop=True).then_inc(gate_done.sem, 1)
                    for name in ("a", "bq", "bk", "cq", "ck"):
                        project(name)

                    pe.wait_ge(*a_read.at(G, 1))
                    for b in range(QB):
                        t = slice(P * b, P * b + P)
                        for n in range(2):
                            r = slice(DK * n, DK * n + DK)
                            last = pe.matmul(score[n][:, t], cum[r, t], qhat[r, t], start=(b == 0), stop=(b == QB - 1), skip_group_check=True)
                    last.then_inc(glaatt_done.sem, 1)
                    for b in range(QB):
                        last = pe.transpose(turn[0][:, P * b:P * b + P], rest[:, P * b:P * b + P], ident[:, :])
                    last.then_inc(kturn_done.sem, 1)
                    project("ag")
                    pe.wait_ge(*kend_ready.at(G, 1))
                    for n in range(NC):
                        r = slice(CH * (n % 2), CH * (n % 2) + CH)
                        dst = (mbank if n % 2 else turn[1])[:, (n // 2) * DV:(n // 2 + 1) * DV]
                        last = pe.matmul(dst, kend[r, n // 2, :], v[r, n // 2, 0:DV], start=(n < 2), stop=(n >= NC - 2), skip_group_check=True)
                    last.then_inc(upd_done.sem, 1)
                    project("bg")

                    def scores(p):
                        if p == 0:
                            pe.wait_ge(*b_parts.at(G, 1))
                            pe.wait_ge(*att_ready.at(G, 1))
                        elif p < 5:
                            pe.wait_ge(*exp_done.at(G, 2 * p))
                        else:
                            pe.wait_ge(*max_ready.at(G, 2 * p))
                        if p == 4:
                            pe.wait_ge(*c_parts.at(G, 1))
                        n, b = p // 4, p % 4
                        q = slice(P * b, P * b + P)
                        for head in range(2):
                            pe.matmul(score[head][:, :], qs[:, 2 * n + head, q], ks[:, 2 * n + head, :], start=True, stop=False)
                        for head in range(2):
                            own = slice(HD * head, HD * head + HD)
                            pe.matmul(score[head][:, :], qs[own, 2 * n + head, q], kl[own, n, :], start=False, stop=True).then_inc(score_done.sem, 1)

                    def turn_weights(u):
                        pe.wait_ge(*w_ready.at(G, u + 1))
                        if u >= 2:
                            pe.wait_ge(*wt_ready.at(G, u - 1))
                        for k in range(QB):
                            last = pe.transpose(turn[u % 2][:, P * k:P * k + P], w[:, u % 2, P * k:P * k + P], ident[:, :])
                        last.then_inc(turn_done.sem, 1)

                    def values(ready, done, *products):
                        pe.wait_ge(*wt_ready.at(G, ready))
                        for k in range(QB):
                            for dst, cols, weights in products:
                                last = pe.matmul(dst, v[:, k, cols], weights[:, k, :], start=(k == 0), stop=(k == QB - 1))
                        last.then_inc(done.sem, 1)

                    scores(0)
                    fill(4)
                    pe.wait_ge(*state_ready.at(G, 1))
                    for b in range(QB):
                        t = slice(P * b, P * b + P)
                        pe.matmul(obank[:, t], v[:, b, 0:DV], attsum[:, t], start=(b == 0), stop=False, skip_group_check=True)
                        for n in (2 * b, 2 * b + 1):
                            t = slice(CH * n, CH * n + CH)
                            last = pe.matmul(obank[:, t], state[:, n, :], qhat[:, t], start=False, stop=(n == NC - 1), skip_group_check=True)
                    last.then_inc(out_done.sem, 1)
                    for u in range(4):
                        scores(u + 1)
                        fill(5)
                        if u == 0:
                            pe.wait_ge(*sq_done.at(G, 1))
                            pe.matmul(mbank[:, :], mean[:, :], sqa[:, :], start=True, stop=True).then_inc(out_done.sem, 1)
                        turn_weights(u)
                    fill(3)
                    values(4, out_done, (obank[:, :], slice(P, 2 * P), wt))
                    for u in range(4, 10):
                        if u % 2 == 0:
                            scores(u // 2 + 3)
                        fill(3 if u in (5, 7) else 4)
                        turn_weights(u)
                        if u == 5:
                            pe.wait_ge(*sq_done.at(G, 2))
                            pe.wait_ge(*y_read.at(G, 2))
                            pe.matmul(obank[:, :], mean[:, :], sqb[:, :], start=True, stop=True).then_inc(out_done.sem, 1)
                    fill(4)
                    turn_weights(10)
                    turn_weights(11)
                    fill(3)
                    assert filled == KT * len(FILLERS)
                    pe.wait_ge(*r_done.at(G, 1))
                    values(12, out_done, (mbank[0:HD, :], slice(2 * P, 2 * P + HD), wt),
                           (mbank[HD:P, :], slice(2 * P + HD, 3 * P), wt1))

                with pe.Fori(0, 2) as half:
                    for c in range(6):
                        pe.wait_ge(*split_done.at(L, half * 6 + (BRANCH_ROW + c + 1)))
                        for is_low in range(2):
                            for zt in (2 * c, 2 * c + 1):
                                if not is_low:
                                    pe.wait_ge(*z_read.at(L, half * 12 + (zt - 5)))
                                for k in range(NG):
                                    n, b = (4 * zt + k) % 8, NG * (zt % 3) + k
                                    if zt < 3:
                                        pe.wait_ge(*(yl_ready.at(L, b + 1) if is_low else high_of_y(L, b)))
                                    for a in (wh,) if is_low else (wh, wl):
                                        last = pe.matmul(zbanks[zt % 6][:, :], a[:, SLOT[c % BRANCH_SLOTS], n, :], (yl if is_low else yh)[:, b, :],
                                                         start=(k == 0 and a is wh and not is_low), stop=(k == NG - 1 and is_low == 1))
                                if is_low:
                                    last.then_inc(tile_done.sem, 1)
                pe.wait_ge(*act_free.at(L + 1, 0))
                for e in range(2):
                    pe.wait_ge(*split_done.at(L, OUT_ROW + e + 1))
                    for k in range(KT - 1):
                        if e == 0:
                            pe.wait_ge(*mixed.at(L, k + 1))
                        product(proj[e][:, :], OUT_SLOT[e % SPLIT], [k])
                pe.wait_ge(*mixed.at(L, KT))
                for e in range(KT):
                    if e >= 2:
                        pe.wait_ge(*split_done.at(L, OUT_ROW + e + 1))
                        pe.wait_ge(*x_ready.at(L, e - 1))
                    product(proj[e % 2][:, :], OUT_SLOT[e % SPLIT], range(KT) if e >= 2 else [KT - 1]).then_inc(tile_done.sem, 1)
                x_mean(L + 1)


def tables():
    half = HD // 2
    inv = (1.0 / THETA ** (np.arange(0, HD, 2, dtype=np.float32) / HD)).astype(np.float32)
    ang = np.arange(S, dtype=np.float32)[:, None] * inv[None, :]
    lane = np.arange(P) % half
    sign = np.where(np.arange(P) % HD < half, -1.0, 1.0).astype(np.float32)
    cos = np.cos(ang)[:, lane].T
    sin = np.sin(ang)[:, lane].T * sign[:, None]
    ahead = np.arange(P)[:, None] + (S - P) - np.arange(2 * S - P)[None, :]
    count = np.zeros(ahead.shape, np.int64)
    for window, dil in PATTERNS:
        count += (ahead % dil == 0) & (np.abs(ahead) // dil <= window // (2 * dil))
    logs = np.where(count > 0, np.log(np.maximum(count, 1)), -1e30).astype(np.float32)
    t = np.arange(S) % CH
    cmask = np.ones((P, S), np.float32)
    cmask[:DK, t == 0] = 0
    cmask[DK:, t == CH - 1] = 0
    a, b = np.arange(P)[:, None], np.arange(P)[None, :]
    same = a // CH == b // CH
    gmask = np.stack([same & (a <= b), same & (a >= b)], 1).astype(np.uint32)
    return [np.ascontiguousarray(t) for t in (cos.astype(np.float32), sin.astype(np.float32), logs, cmask, gmask,
                                              np.eye(P, dtype=np.float32))]


def columns():
    names = ["aq", "ak", "av", "ag", "lf", "lb", "bq", "bk", "bv", "bg", "cq", "ck", "cv", "cg", "m"]
    widths = [256, 256, 512, 512, 16, 16] + [512] * 8 + [3072]
    starts = np.cumsum([0] + widths[:-1])
    return dict(zip(names, starts.tolist()))


def stream(w_in, w_branch, w_out):
    at = columns()
    w_in = w_in.reshape(DEPTH, KT, P, -1)
    order = []
    for i in range(NG):
        for name in VALUES:
            order.append(np.arange(P) + at[name] + P * i)
        for name in UNIT_TILES:
            if name == "a":
                order.append(np.concatenate([np.arange(DK) + at[t] + DK * i for t in ("aq", "ak")]))
            elif name[0] == "m":
                n = 6 * i + int(name[1])
                order.append(np.arange(P) + at["m"] + (n % 3) * D + (n // 3) * P)
            else:
                order.append(np.arange(P) + at[name] + P * i)
    out = np.empty((DEPTH, ROWS_LAYER, P, 8, P), np.float32)
    for i in range(NG):
        for u, cols in enumerate(order[GU * i:GU * i + GU]):
            out[:, 1 + GU * i + u] = w_in[:, :, :, cols].transpose(0, 2, 1, 3)
    out[:, 0] = 0
    out[:, 0, :, :, :2 * RANK] = w_in[:, :, :, at["lf"]:at["lf"] + 2 * RANK].transpose(0, 2, 1, 3)
    wb = w_branch.reshape(DEPTH, 3, NG, P, KT, P).transpose(0, 4, 1, 2, 3, 5).reshape(DEPTH, 12, 8, P, P)
    out[:, BRANCH_ROW:OUT_ROW] = wb.transpose(0, 1, 3, 2, 4)
    out[:, OUT_ROW:] = w_out.reshape(DEPTH, KT, P, KT, P).transpose(0, 3, 2, 1, 4)
    return out.reshape(DEPTH * ROWS_LAYER, P, 8 * P)


def decay_projections(gate_up, gate_b):
    out = np.zeros((DEPTH, NG, P, P + 1), np.float32)
    for hd in range(NG):
        for d in range(2):
            c = DK * d
            out[:, hd, RANK * d:RANK * d + RANK, c:c + DK] = gate_up[:, d, :, DK * hd:DK * hd + DK]
            out[:, hd, c:c + DK, P] = gate_b[:, d, DK * hd:DK * hd + DK]
    return out.reshape(DEPTH * NG, P, P + 1)


def parameters(norm_g, gla_g, diff_lambda, diff_g):
    out = np.zeros((DEPTH, P, NPAR), np.float32)
    out[:, :, C_NG:C_NG + KT] = norm_g.reshape(DEPTH, KT, P).transpose(0, 2, 1)
    out[:, :, C_GA] = gla_g
    out[:, :, C_GD] = diff_g
    out[:, :, C_DL:C_DL + 4 * HD] = diff_lambda.reshape(DEPTH, 1, -1)
    for layer in range(DEPTH):
        init = 0.8 - 0.6 * math.exp(-0.3 * layer)
        out[layer, :, C_LI] = init
        out[layer, :, C_LI + 1] = 1.0 - init
    return out


def kernel(x, norm_g, w_in, gla_gate_up, gla_gate_b, gla_norm_g, diff_lambda, diff_norm_g, w_branch, w_out, final_norm_g):
    import concourse.bacc as bacc
    from concourse.bass_utils import run_bass_kernel_spmd as run

    x, norm_g, w_in, gla_gate_up, gla_gate_b, gla_norm_g, diff_lambda, diff_norm_g, w_branch, w_out, final_norm_g = (
        np.asarray(a) for a in (x, norm_g, w_in, gla_gate_up, gla_gate_b, gla_norm_g, diff_lambda, diff_norm_g, w_branch,
                                w_out, final_norm_g))
    cos, sin, lmask, cmask, gmask, ident = tables()
    arrays = {
        "x_t": np.ascontiguousarray(x.reshape(S, KT, P).transpose(2, 1, 0)),
        "weights": stream(w_in, w_branch, w_out),
        "params": parameters(norm_g, gla_norm_g, diff_lambda, diff_norm_g),
        "decay_w": decay_projections(gla_gate_up, gla_gate_b),
        "final_g": np.ascontiguousarray(final_norm_g.reshape(KT, P).T),
        "cos_t": cos, "sin_t": sin, "lmask_t": lmask, "cmask_t": cmask, "gmask_t": gmask, "ident_t": ident,
    }
    nc = bacc.Bacc("TRN2", target_bir_lowering=False, num_devices=1)
    args = [nc.dram_tensor(n, a.shape, mybir.dt.from_np(a.dtype), kind="ExternalInput").ap() for n, a in arrays.items()]
    out = nc.dram_tensor("out_t", (P, KT, S), F32, kind="ExternalOutput").ap()
    gate_scratch = nc.dram_tensor("gate_scratch", (3 * KT, P, S), F32, kind="Internal").ap()
    x_scratch = nc.dram_tensor("x_scratch", (P, KT, S), F32, kind="Internal").ap()
    build(nc, *args, out, gate_scratch, x_scratch)
    r = run(nc, [arrays], core_ids=[0])
    return np.ascontiguousarray(r.results[0]["out_t"].transpose(2, 1, 0)).reshape(1, S, D)
```
